# Optimizing a Trainium2 kernel written in Bass

```python
import math
import jax, jax.numpy as jnp
from jax import lax
import numpy as np

D_MODEL = 1024
BATCH = 1
SEQ = 512
DEPTH = 1

MEM_LEN = 256
MLA_HEADS = 8
MLA_Q_RANK = 256
MLA_KV_RANK = 128
MLA_NOPE = 64
MLA_ROPE = 32
MLA_V = 64
ROPE_THETA = 10000.0
SB_HEADS = 8
SB_HEAD_DIM = 64
X_HEADS = 4
X_HEAD_DIM = 128
D_FF = -(-8 * D_MODEL // (3 * 256)) * 256
Q_BLOCK = 128
EPS = 1e-6
SB_WIDTH = SB_HEADS * SB_HEAD_DIM
IN_SPLITS = (MLA_Q_RANK, MLA_KV_RANK, MLA_ROPE, SB_WIDTH, SB_WIDTH, SB_WIDTH, D_MODEL, D_MODEL)
D_IN = MLA_Q_RANK + MLA_KV_RANK + MLA_ROPE + 3 * SB_WIDTH + 2 * D_MODEL

kernel_name = "hybrid_mla_stickbreaking_gated_block"

def rms_norm(x, g):
    xf = x.astype(jnp.float32)
    y = xf * lax.rsqrt(jnp.mean(xf * xf, axis=-1, keepdims=True) + EPS)
    return (y * g.astype(jnp.float32)).astype(x.dtype)

def rope_cos_sin(positions):
    inv_freq = ROPE_THETA ** (-jnp.arange(0, MLA_ROPE, 2, dtype=jnp.float32) / MLA_ROPE)
    ang = positions.astype(jnp.float32)[..., None] * inv_freq
    return jnp.cos(ang), jnp.sin(ang)

def apply_rope(x, cos, sin):
    half = x.shape[-1] // 2
    x1 = x[..., :half].astype(jnp.float32)
    x2 = x[..., half:].astype(jnp.float32)
    out = jnp.concatenate([x1 * cos - x2 * sin, x2 * cos + x1 * sin], axis=-1)
    return out.astype(x.dtype)

def mla_block(qb, blk, k, v):
    scale = 1.0 / math.sqrt(MLA_NOPE + MLA_ROPE)
    s = jnp.einsum('bqhd,bkhd->bhqk', qb, k).astype(jnp.float32) * scale
    q_pos = blk * Q_BLOCK + jnp.arange(Q_BLOCK)
    k_pos = jnp.arange(k.shape[1])
    mask = k_pos[None, :] <= q_pos[:, None]
    s = jnp.where(mask, s, jnp.finfo(jnp.float32).min)
    p = jax.nn.softmax(s, axis=-1).astype(v.dtype)
    return jnp.einsum('bhqk,bkhd->bqhd', p, v)

def stick_breaking_block(qb, blk, k, v):
    scale = 1.0 / math.sqrt(SB_HEAD_DIM)
    z = jnp.einsum('bqhd,bkhd->bhqk', qb, k).astype(jnp.float32) * scale
    q_pos = blk * Q_BLOCK + jnp.arange(Q_BLOCK)
    k_pos = jnp.arange(k.shape[1])
    mask = k_pos[None, :] < q_pos[:, None]
    log_beta = jax.nn.log_sigmoid(z)
    log_one_minus = jnp.where(mask, jax.nn.log_sigmoid(-z), 0.0)
    suffix = lax.cumsum(log_one_minus, axis=3, reverse=True) - log_one_minus
    a = jnp.where(mask, jnp.exp(log_beta + suffix), 0.0).astype(v.dtype)
    return jnp.einsum('bhqk,bkhd->bqhd', a, v)

def blocked_attend(block_fn, q, k, v):
    b, s, h, dq = q.shape
    dv = v.shape[-1]
    nb = s // Q_BLOCK
    qb = q.reshape(b, nb, Q_BLOCK, h, dq).transpose(1, 0, 2, 3, 4)
    out = lax.map(lambda a: block_fn(a[0], a[1], k, v), (qb, jnp.arange(nb)))
    return out.transpose(1, 0, 2, 3, 4).reshape(b, s, h * dv)

def setup_inputs(seed: int = 0) -> dict:
    key = jax.random.key(seed)
    ks = jax.random.split(key, 24)

    def w(k, shape, fan_in):
        return jax.random.normal(k, shape, jnp.float32) * (fan_in ** -0.5)

    def gain(k, shape):
        return 1.0 + 0.01 * jax.random.normal(k, shape, jnp.float32)

    L = DEPTH
    return {
        "x": jax.random.normal(ks[0], (BATCH, SEQ, D_MODEL), jnp.float32),
        "mem": jax.random.normal(ks[1], (BATCH, MEM_LEN, D_MODEL), jnp.float32),
        "positions": jnp.broadcast_to(jnp.arange(SEQ, dtype=jnp.int32)[None, :], (BATCH, SEQ)),
        "g_mix": gain(ks[2], (L, D_MODEL)),
        "w_in": w(ks[3], (L, D_MODEL, D_IN), D_MODEL),
        "b_gate": 0.01 * jax.random.normal(ks[4], (L, 2, D_MODEL), jnp.float32),
        "g_q_lat": gain(ks[5], (L, MLA_Q_RANK)),
        "w_uq": w(ks[6], (L, MLA_Q_RANK, MLA_HEADS * (MLA_NOPE + MLA_ROPE)), MLA_Q_RANK),
        "g_kv_lat": gain(ks[7], (L, MLA_KV_RANK)),
        "w_ukv": w(ks[8], (L, MLA_KV_RANK, MLA_HEADS * (MLA_NOPE + MLA_V)), MLA_KV_RANK),
        "w_a_proj": w(ks[9], (L, MLA_HEADS * MLA_V, D_MODEL), MLA_HEADS * MLA_V),
        "w_b_proj": w(ks[10], (L, SB_WIDTH, D_MODEL), SB_WIDTH),
        "w_o": w(ks[11], (L, D_MODEL, D_MODEL), D_MODEL),
        "g_x": gain(ks[12], (L, D_MODEL)),
        "g_mem": gain(ks[13], (L, D_MODEL)),
        "w_xq": w(ks[14], (L, D_MODEL, X_HEADS * X_HEAD_DIM), D_MODEL),
        "w_xkv": w(ks[15], (L, D_MODEL, 2 * X_HEADS * X_HEAD_DIM), D_MODEL),
        "w_xo": w(ks[16], (L, X_HEADS * X_HEAD_DIM, D_MODEL), X_HEADS * X_HEAD_DIM),
        "g_ffn": gain(ks[17], (L, D_MODEL)),
        "w_gate": w(ks[18], (L, D_MODEL, D_FF), D_MODEL),
        "w_up": w(ks[19], (L, D_MODEL, D_FF), D_MODEL),
        "w_down": w(ks[20], (L, D_FF, D_MODEL), D_FF),
        "g_final": gain(ks[21], (D_MODEL,)),
    }

def reference(x, mem, positions, g_mix, w_in, b_gate, g_q_lat, w_uq, g_kv_lat, w_ukv,
              w_a_proj, w_b_proj, w_o, g_x, g_mem, w_xq, w_xkv, w_xo,
              g_ffn, w_gate, w_up, w_down, g_final):
    b, s, _ = x.shape
    m_len = mem.shape[1]
    cos, sin = rope_cos_sin(positions)
    split_points = list(np.cumsum(IN_SPLITS)[:-1])

    for l in range(DEPTH):
        h = rms_norm(x, g_mix[l])
        proj = h @ w_in[l]
        c_q, c_kv, k_r, sb_q, sb_k, sb_v, gate_a, gate_b = jnp.split(proj, split_points, axis=-1)

        q = (rms_norm(c_q, g_q_lat[l]) @ w_uq[l]).reshape(b, s, MLA_HEADS, MLA_NOPE + MLA_ROPE)
        q_rope = apply_rope(q[..., MLA_NOPE:], cos[:, :, None, :], sin[:, :, None, :])
        q_a = jnp.concatenate([q[..., :MLA_NOPE], q_rope], axis=-1)
        kv = (rms_norm(c_kv, g_kv_lat[l]) @ w_ukv[l]).reshape(b, s, MLA_HEADS, MLA_NOPE + MLA_V)
        k_r = apply_rope(k_r, cos, sin)
        k_a = jnp.concatenate(
            [kv[..., :MLA_NOPE], jnp.broadcast_to(k_r[:, :, None, :], (b, s, MLA_HEADS, MLA_ROPE))], axis=-1)
        v_a = kv[..., MLA_NOPE:]
        o_a = blocked_attend(mla_block, q_a, k_a, v_a)

        o_b = blocked_attend(
            stick_breaking_block,
            sb_q.reshape(b, s, SB_HEADS, SB_HEAD_DIM),
            sb_k.reshape(b, s, SB_HEADS, SB_HEAD_DIM),
            sb_v.reshape(b, s, SB_HEADS, SB_HEAD_DIM))

        merged = (jax.nn.sigmoid(gate_a + b_gate[l, 0]) * (o_a @ w_a_proj[l])
                  + jax.nn.sigmoid(gate_b + b_gate[l, 1]) * (o_b @ w_b_proj[l]))
        x = x + merged @ w_o[l]

        hx = rms_norm(x, g_x[l])
        mn = rms_norm(mem, g_mem[l])
        xq = (hx @ w_xq[l]).reshape(b, s, X_HEADS, X_HEAD_DIM)
        xkv = (mn @ w_xkv[l]).reshape(b, m_len, 2, X_HEADS, X_HEAD_DIM)
        xs = jnp.einsum('bqhd,bkhd->bhqk', xq, xkv[:, :, 0]).astype(jnp.float32) / math.sqrt(X_HEAD_DIM)
        xp = jax.nn.softmax(xs, axis=-1).astype(x.dtype)
        xo = jnp.einsum('bhqk,bkhd->bqhd', xp, xkv[:, :, 1]).reshape(b, s, X_HEADS * X_HEAD_DIM)
        x = x + xo @ w_xo[l]

        hf = rms_norm(x, g_ffn[l])
        x = x + (jax.nn.silu(hf @ w_gate[l]) * (hf @ w_up[l])) @ w_down[l]

    return rms_norm(x, g_final)


_drawn_inputs = setup_inputs


def setup_inputs(seed=0):
    import zlib

    import numpy as np

    out = dict(_drawn_inputs(seed))
    spreads = {}
    factors = {'g_mix': 8.0,
     'b_gate': 8.0,
     'g_q_lat': 8.0,
     'g_kv_lat': 8.0,
     'g_x': 8.0,
     'g_mem': 8.0,
     'g_ffn': 8.0,
     'g_final': 5.482}
    for name, (base, spread) in spreads.items():
        noise = np.random.default_rng([zlib.crc32(name.encode()), seed]).standard_normal(out[name].shape)
        drawn = base * np.exp(spread * noise) if base else spread * noise
        out[name] = __import__('jax').numpy.asarray(drawn.astype(out[name].dtype))
    for name, factor in factors.items():
        out[name] = (out[name] * factor).astype(out[name].dtype)
    return out
```

```python
from contextlib import ExitStack

import concourse.bass as bass
import numpy as np
from concourse import mybir
from concourse.alu_op_type import AluOpType as ALU

F32 = mybir.dt.float32
F32R = mybir.dt.float32r
I32 = mybir.dt.int32
ACT = mybir.ActivationFunctionType
AX_X = mybir.AxisListType.X

P = 128
S = 512
D = 1024
KD = D // P
MEM = 256
NH = 8
NOPE, ROPE, DV = 64, 32, 64
QK = NOPE + ROPE
QR, KVR = 256, 128
SBH, SBD = 8, 64
XH, XD = 4, 128
FF = 2816
KF = FF // P
EPS = 1e-6
MLA_SCALE = QK ** -0.5
SB_SCALE = SBD ** -0.5
X_SCALE = XD ** -0.5
NEG = -1.0e30
HALF_PI = float(np.pi / 2)
KB = 1024
NT = S // P

C_CQ, C_CKV, C_KR = 0, QR, QR + KVR
C_SBQ = C_KR + ROPE
C_SBK = C_SBQ + SBH * SBD
C_SBV = C_SBK + SBH * SBD
C_GA = C_SBV + SBH * SBD

U_CQ, U_SB, U_GATE, U_MERGE, U_WO, U_XV, U_XKQ, U_XO, U_FFN, U_DOWN, U_END = (
    0, 4, 16, 32, 40, 48, 52, 60, 64, 108, 132)
G_CQ, G_SB, G_GATE, G_MERGE, G_WO, G_XKQ, G_XO, G_FFN, G_DOWN, G_END = (
    0, 4, 16, 32, 48, 56, 64, 72, 116, 124)
SB_FIRST = 2
SB_FILL = (2, 1, 1, 1, 2, 1, 1, 1)
Q_X, Q_CQ, Q_CKV, Q_X2, Q_X3, Q_X4 = 0, 8, 10, 11, 19, 27
N_X, N_CQ, N_CKV, N_X2, N_X3, N_X4 = 0, 1, 2, 3, 4, 5
Q0 = (0, 128, 256, 256)
OFF = (0, 512, 896, 1152)
CAUSAL = 1408
PT_STEP = 384
DOWN_K = (8, 8, 6)
R_MIX, R_X, R_MEM, R_FFN, R_FINAL, R_BIAS, R_Q, R_KV, R_ALL = 0, 8, 16, 24, 32, 40, 56, 58, 59


def build(nc, x, mem, positions, g_mix, w_in, b_gate, g_q_lat, w_uq, g_kv_lat, w_ukv, w_a_proj,
          w_b_proj, w_o, g_x, g_mem, w_xq, w_xkv, w_xo, g_ffn, w_gate, w_up, w_down, g_final,
          signed_freq, out):
    with ExitStack() as ctx:
        arena0 = 16512

        def sb(name, shape, dt, at):
            size = int(np.prod(shape[1:])) * 4
            assert arena0 + at + size <= 229344, (name, at, size)
            return nc.alloc_sbuf_tensor_at(name, shape, dt, offset=arena0 + at)

        def sem(name):
            return ctx.enter_context(nc.semaphore(name))

        h_hi = sb("h_hi", [P, KD, S], F32R, 0)
        h_lo = sb("h_lo", [P, KD, S], F32R, 16 * KB)
        xT = sb("xT", [P, KD, S], F32, 32 * KB)
        raw = [sb(f"raw{s}", [P, 1024], F32, (48 + 4 * s) * KB) for s in range(2)]
        w_hi = [sb(f"w_hi{s}", [P, 1024], F32R, (56 + 8 * s) * KB) for s in range(2)]
        w_lo = [sb(f"w_lo{s}", [P, 1024], F32R, (60 + 8 * s) * KB) for s in range(2)]
        fixed = [72 * KB]

        def small(name, cols, dt=F32):
            at = fixed[0]
            fixed[0] += (cols * 4 + 31) // 32 * 32
            assert fixed[0] <= 84 * KB
            return sb(name, [P, cols], dt, at)

        rs = small("rs", S)
        sq_sum = small("sq_sum", S)
        sq_tile = small("sq_tile", S)
        mask_row = small("mask_row", S)
        ident = small("ident", P)
        mask_kq = small("mask_kq", P)
        neg_tri = small("neg_tri", P, F32R)
        neg_ones = small("neg_ones", P, F32R)
        ones = small("ones", P)
        gains = small("gains", 64)
        consts = small("consts", 8)
        stat = small("stat", 16)
        stat_x = small("stat_x", 32)
        eps_c, half_pi_c, one_c = consts[:, 0:1], consts[:, 1:2], consts[:, 2:3]
        A0 = 84 * KB

        def area(name, shape, dt, kb):
            return sb(name, shape, dt, A0 + int(kb * KB))

        x_nat = area("x_nat", [P, NT, D], F32, 91)
        gain_rows = area("gain_rows", [P, P], F32, 32)
        scratch = area("scratch", [P, P], F32, 33)
        c_raw = area("c_raw", [P, 4, S], F32, 91)
        wu_raw = area("wu_raw", [P, 2560], F32, 107)
        cq_hi = area("cq_hi", [P, 2, S], F32R, 0)
        cq_lo = area("cq_lo", [P, 2, S], F32R, 4)
        ckv_hi = area("ckv_hi", [P, S], F32R, 8)
        ckv_lo = area("ckv_lo", [P, S], F32R, 10)
        wu_hi = area("wu_hi", [P, 2560], F32R, 12)
        wu_lo = area("wu_lo", [P, 2560], F32R, 22)
        q_hi = [area(f"q_hi{b}", [P, S], F32R, 32 + 4 * b) for b in range(2)]
        q_lo = [area(f"q_lo{b}", [P, S], F32R, 34 + 4 * b) for b in range(2)]
        k_hi = [area(f"k_hi{b}", [P, S], F32R, 40 + 4 * b) for b in range(2)]
        k_lo = [area(f"k_lo{b}", [P, S], F32R, 42 + 4 * b) for b in range(2)]
        va_hi = area("va_hi", [P, NT, S], F32R, 48)
        va_lo = area("va_lo", [P, NT, S], F32R, 56)
        probs = area("probs", [P, 1280], F32, 64)
        pT = area("pT", [P, 3584], F32R, 69)
        cos_t = area("cos_t", [P, S], F32, 83)
        sin_t = area("sin_t", [P, S], F32, 85)
        swapped = area("swapped", [P, S], F32, 87)
        roped = area("roped", [P, S], F32, 89)
        ang = area("ang", [P, S], F32, 64)
        turns = area("turns", [P, S], F32, 66)
        pos_i = area("pos_i", [P, S], I32, 69)
        rs_c = [area(f"rs_c{n}", [P, S], F32, 71 + 2 * n) for n in range(2)]
        c_norm = area("c_norm", [P, S], F32, 75)
        sbq = area("sbq", [P, 4, S], F32, 91)
        sbk = area("sbk", [P, 4, S], F32, 99)
        sbvT = area("sbvT", [P, 4, S], F32, 107)
        oa = area("oa", [P, 4, S], F32, 115)
        vb_hi = area("vb_hi", [P, NT, S], F32R, 0)
        vb_lo = area("vb_lo", [P, NT, S], F32R, 8)
        qs_hi = [area(f"qs_hi{b}", [P, S], F32R, 16 + 4 * b) for b in range(2)]
        qs_lo = [area(f"qs_lo{b}", [P, S], F32R, 18 + 4 * b) for b in range(2)]
        ks_hi = [area(f"ks_hi{b}", [P, S], F32R, (24, 87)[b]) for b in range(2)]
        ks_lo = [area(f"ks_lo{b}", [P, S], F32R, (26, 89)[b]) for b in range(2)]
        stick = area("stick", [P, 1280], F32, 28)
        sp_hi = area("sp_hi", [P, CAUSAL], F32R, 33)
        sp_lo = area("sp_lo", [P, CAUSAL], F32R, 38.5)
        a_hi = area("a_hi", [P, CAUSAL], F32R, 44)
        a_lo = area("a_lo", [P, CAUSAL], F32R, 49.5)
        gates = area("gates", [P, 16, S], F32, 55)
        oa_hi = area("oa_hi", [P, 4, S], F32R, 99)
        oa_lo = area("oa_lo", [P, 4, S], F32R, 115)
        ob_hi = area("ob_hi", [P, 4, S], F32R, 107)
        ob_lo = area("ob_lo", [P, 4, S], F32R, 91)
        m_hi = area("m_hi", [P, KD, S], F32R, 32)
        m_lo = area("m_lo", [P, KD, S], F32R, 55)
        gated = [area(f"gated{b}", [P, S], F32, 87 + 2 * b) for b in range(2)]
        mem_nat = area("mem_nat", [P, 2, D], F32, 16)
        mem_junk = area("mem_junk", [P, D], F32, 24)
        mn_hi = area("mn_hi", [P, KD, MEM], F32R, 0)
        mn_lo = area("mn_lo", [P, KD, MEM], F32R, 8)
        xk_hi = area("xk_hi", [P, 4, MEM], F32R, 24)
        xk_lo = area("xk_lo", [P, 4, MEM], F32R, 28)
        xv_hi = area("xv_hi", [P, 2, S], F32R, 56)
        xv_lo = area("xv_lo", [P, 2, S], F32R, 60)
        xq_hi = area("xq_hi", [P, 4, S], F32R, 64)
        xq_lo = area("xq_lo", [P, 4, S], F32R, 72)
        xq_raw = [area(f"xq_raw{b}", [P, S], F32, 80 + 2 * b) for b in range(2)]
        xp = [area(f"xp{b}", [P, 4, MEM], F32, (84, 115)[b]) for b in range(2)]
        xpT_hi = area("xpT_hi", [P, 2, S], F32R, 16)
        xpT_lo = area("xpT_lo", [P, 2, S], F32R, 20)
        xo_hi = area("xo_hi", [P, 4, S], F32R, 91)
        xo_lo = area("xo_lo", [P, 4, S], F32R, 99)
        f_hi = area("f_hi", [P, KF, S], F32R, 0)
        f_lo = area("f_lo", [P, KF, S], F32R, 44)
        g_t = [area(f"g_t{b}", [P, S], F32, 107 + 2 * b) for b in range(2)]
        u_t = [area(f"u_t{b}", [P, S], F32, 111 + 2 * b) for b in range(2)]
        yT = area("yT", [P, 4, S], F32, 88)
        y_nat = area("y_nat", [P, NT, D], F32, 104)

        ps = [ctx.enter_context(nc.psum_tensor(f"ps{b}", [P, S], F32)) for b in range(8)]

        raw_in = [sem(f"raw_in{s}") for s in range(2)]
        hi_done = sem("hi_done")
        lo_done = sem("lo_done")
        unit_done = sem("unit_done")
        evac = sem("evac")
        x_in = [sem(f"x_in{t}") for t in range(NT)]
        gains_in, pos_in, wu_in, mem_in, y_out = map(sem, ("gains_in", "pos_in", "wu_in", "mem_in", "y_out"))
        pool_const = sem("pool_const")
        const_r = sem("const_r")
        gains_T, gains_ok = sem("gains_T"), sem("gains_ok")
        x_T = sem("x_T")
        x_kept = sem("x_kept")
        h_hi_ok, h_lo_ok = sem("h_hi_ok"), sem("h_lo_ok")
        sq_ok, sq_added = sem("sq_ok"), sem("sq_added")
        sum_clear = sem("sum_clear")
        stat_ok, rs_ok = sem("stat_ok"), sem("rs_ok")
        ln_ok = sem("ln_ok")
        freq_in = sem("freq_in")
        trig_arg, trig_ok = sem("trig_arg"), sem("trig_ok")
        dve_step, act_step, pool_step = sem("dve_step"), sem("act_step"), sem("pool_step")
        wu_hi_ok, wu_lo_ok = sem("wu_hi_ok"), sem("wu_lo_ok")
        cn_ok, c_hi_ok, c_lo_ok = sem("cn_ok"), sem("c_hi_ok"), sem("c_lo_ok")
        kr_ok, kr_hi_ok, kr_lo_ok = sem("kr_ok"), sem("kr_hi_ok"), sem("kr_lo_ok")
        va_mm, va_hi_ok, va_lo_ok = sem("va_mm"), sem("va_hi_ok"), sem("va_lo_ok")
        proj_mm = sem("proj_mm")
        dve_rope = sem("dve_rope")
        rope_ok, qk_hi_ok, qk_lo_ok = sem("rope_ok"), sem("qk_hi_ok"), sem("qk_lo_ok")
        s_mm, s_ok, e_ok, p_ok = sem("s_mm"), sem("s_ok"), sem("e_ok"), sem("p_ok")
        t_mm, pt_hi_ok, pt_lo_ok = sem("t_mm"), sem("pt_hi_ok"), sem("pt_lo_ok")
        pv_mm, o_ok = sem("pv_mm"), sem("o_ok")
        zero_ok = sem("zero_ok")
        vT_mm, vb_hi_ok, vb_lo_ok = sem("vT_mm"), sem("vb_hi_ok"), sem("vb_lo_ok")
        sq_stage_hi, sq_stage_lo = sem("sq_stage_hi"), sem("sq_stage_lo")
        z_mm, z_ok, l_ok, sp_ok, sp_hi_ok, sp_lo_ok = map(sem, ("z_mm", "z_ok", "l_ok", "sp_ok", "sp_hi_ok", "sp_lo_ok"))
        w_mm, a_ok, a_hi_ok, a_lo_ok = sem("w_mm"), sem("a_ok"), sem("a_hi_ok"), sem("a_lo_ok")
        pvb_mm, ob_hi_ok, ob_ok = sem("pvb_mm"), sem("ob_hi_ok"), sem("ob_ok")
        sig_ok, oa_hi_ok, oa_lo_ok = sem("sig_ok"), sem("oa_hi_ok"), sem("oa_lo_ok")
        m_ok, m_hi_ok, m_lo_ok = sem("m_ok"), sem("m_hi_ok"), sem("m_lo_ok")
        mem_sq, mem_rs = sem("mem_sq"), sem("mem_rs")
        mem_n, mem_T, mn_hi_ok, mn_lo_ok = sem("mem_n"), sem("mem_T"), sem("mn_hi_ok"), sem("mn_lo_ok")
        xv_hi_ok, xv_lo_ok, xk_hi_ok = sem("xv_hi_ok"), sem("xv_lo_ok"), sem("xk_hi_ok")
        xo_mm = sem("xo_mm")
        xq_hi_ok, xq_lo_ok = sem("xq_hi_ok"), sem("xq_lo_ok")
        xs_mm, xs_max, xe_ok, xp_ok = sem("xs_mm"), sem("xs_max"), sem("xe_ok"), sem("xp_ok")
        xt_mm, xt_hi_ok, xt_lo_ok = sem("xt_mm"), sem("xt_hi_ok"), sem("xt_lo_ok")
        xpv_mm, xo_hi_ok, xo_lo_ok = sem("xpv_mm"), sem("xo_hi_ok"), sem("xo_lo_ok")
        silu_ok, f_ok, f_hi_ok, f_lo_ok = sem("silu_ok"), sem("f_ok"), sem("f_hi_ok"), sem("f_lo_ok")
        y_ok, yT_mm, y_rs, y_left, y_right = map(sem, ("y_ok", "yT_mm", "y_rs", "y_left", "y_right"))

        def fl(ap):
            return ap.bitcast(F32)

        def tile(t, m, n=1):
            return t[:, m:m + n, :] if isinstance(m, int) else t[:, bass.ds(m, n), :]

        def col(t, m):
            return t[:, m:m + 1] if isinstance(m, int) else t[:, bass.ds(m, 1)]

        def bank(b, n=1, w=S):
            return ps[b][:, 0:w].rearrange("p (a n) -> p a n", a=n)

        def cols(base, m, w=P):
            return base[:, :, m:m + w] if isinstance(m, int) else base[:, :, bass.ds(m, w)]

        def repeat(eng, first, n, body):
            with eng.Fori(first, first + n) as i:
                body(i)

        class Steps:

            def __init__(self, eng, s):
                self.eng, self.sem, self.n, self.off = eng, s, 0, 0

            def link(self, ins):
                ins.then_inc(self.sem, 1)
                self.n += 1
                self.eng.wait_ge(self.sem, self.n + self.off)

            def repeat(self, first, n, body, per):
                at = self.n
                with self.eng.Fori(first, first + n) as i:
                    self.off = (i - first) * per
                    body(i)
                assert self.n - at == per
                self.n, self.off = at + per * n, 0

        w_in_v = w_in[0].rearrange("(k p) n -> p k n", p=P)

        fills, u = [], U_SB + SB_FIRST
        for n in SB_FILL:
            fills.append(([u], [u + 1] if n == 2 else []))
            u += n
        assert u == U_GATE

        block = ctx.enter_context(nc.Block())

        @block.sync
        def _(sp):
            def load(u, s, src, n, first=False):
                if not first:
                    sp.wait_ge(lo_done, u - 1)
                sp.dma_start(raw[s][:, 0:n], src).then_inc(raw_in[s], 16)

            def load3(u, s, src, k, first=False):
                if not first:
                    sp.wait_ge(lo_done, u - 1)
                w = src.shape[2]
                sp.dma_start(raw[s][:, 0:k * w].rearrange("p (k n) -> p k n", k=k), src).then_inc(raw_in[s], 16)

            load3(0, 0, cols(w_in_v, 0), KD, first=True)
            load3(1, 1, cols(w_in_v, P), KD, first=True)
            load3(2, 0, cols(w_in_v, C_CKV), KD)
            load3(3, 1, cols(w_in_v, C_KR - NOPE, QK), KD)

            def in_pair(i):
                for s in range(2):
                    load3(U_SB + 2 * i + s, s, cols(w_in_v, C_SBQ + 2 * P * i + P * s), KD)
            repeat(sp, 0, (U_MERGE - U_SB) // 2, in_pair)

            a_v = w_a_proj[0].rearrange("(k p) n -> p k n", p=P)
            b_v = w_b_proj[0].rearrange("(k p) n -> p k n", p=P)

            def merge(t):
                load3(U_MERGE + 2 * t, 0, cols(a_v, 2 * P * t, 2 * P), 4)
                load3(U_MERGE + 2 * t + 1, 1, cols(b_v, 2 * P * t, 2 * P), 4)
            repeat(sp, 0, 4, merge)

            def square(base, w):
                v = w[0].rearrange("(k p) n -> p k n", p=P)

                def body(i):
                    for s in range(2):
                        load3(base + 2 * i + s, s, cols(v, 2 * P * i + P * s), KD)
                return body
            repeat(sp, 0, 4, square(U_WO, w_o))
            xkv_v = w_xkv[0].rearrange("(k p) n -> p k n", p=P)
            xq_v = w_xq[0].rearrange("(k p) n -> p k n", p=P)
            for j in range(4):
                load3(U_XV + j, j % 2, xkv_v[:, 2 * j:2 * j + 2, XH * XD:2 * XH * XD], 2)

            def x_head(h):
                load3(U_XKQ + 2 * h, 0, cols(xkv_v, XD * h), KD)
                load3(U_XKQ + 2 * h + 1, 1, cols(xq_v, XD * h), KD)
            repeat(sp, 0, XH, x_head)
            xo_v = w_xo[0].rearrange("(k p) n -> p k n", p=P)

            def xo_pair(i):
                for s in range(2):
                    load3(U_XO + 2 * i + s, s, cols(xo_v, 4 * P * i + 2 * P * s, 2 * P), 4)
            repeat(sp, 0, 2, xo_pair)
            gate_v = w_gate[0].rearrange("(k p) n -> p k n", p=P)
            up_v = w_up[0].rearrange("(k p) n -> p k n", p=P)

            def ffn(m):
                load3(U_FFN + 2 * m, 0, cols(gate_v, P * m), KD)
                load3(U_FFN + 2 * m + 1, 1, cols(up_v, P * m), KD)
            repeat(sp, 0, KF, ffn)
            down_v = w_down[0].rearrange("(k p) n -> p k n", p=P)

            def down(i):
                for j in range(6):
                    k0 = sum(DOWN_K[:j % 3])
                    k = DOWN_K[j % 3]
                    load3(U_DOWN + 6 * i + j, j % 2, cols(down_v[:, k0:k0 + k, :], 2 * P * i + P * (j // 3)), k)
            repeat(sp, 0, 4, down)

            for t in range(NT):
                sp.wait_ge(y_left, t + 1)
                sp.wait_ge(y_right, t + 1)
                sp.dma_start(out[0, t * P:(t + 1) * P, :], y_nat[:, t, :]).then_inc(y_out, 16)
            sp.wait_ge(y_out, 16 * NT)

        @block.tensor
        def _(pe):
            def three(acc, l_hi, l_lo, r_hi, r_lo, start, stop):
                pe.matmul(acc, l_hi, r_hi, start=start, stop=False)
                pe.matmul(acc, l_hi, r_lo, start=False, stop=False)
                return pe.matmul(acc, l_lo, r_hi, start=False, stop=stop)

            def gemm(u, s, banks, kts, r_hi, r_lo, width=P, n=S, start=True, stop=True, k0=0, ready=None, free=None):
                pe.wait_ge(lo_done, u + 1)
                m = len(banks)
                for b, dst in enumerate(banks):
                    if free:
                        free(b)
                    for k in range(kts):
                        if ready and b == 0:
                            ready(k)
                        c = (k * m + b) * width
                        last = three(ps[dst][0:width, 0:n], w_hi[s][:, c:c + width], w_lo[s][:, c:c + width],
                                     r_hi[:, k0 + k, :], r_lo[:, k0 + k, :],
                                     start and k == 0, stop and k == kts - 1)
                last.then_inc(unit_done, 1)

            def statistic(n, squares):
                pe.wait_ge(sq_added, squares)
                pe.matmul(ps[7][:, :], ones[:, :], sq_sum[:, :], start=True, stop=True).then_inc(stat_ok, 1)

            pe.wait_ge(pool_const, 4)
            pe.wait_ge(gains_in, 16 * 8)
            pe.transpose(ps[7][:, 0:R_ALL], gain_rows[0:R_ALL, :], ident[0:R_ALL, 0:R_ALL]).then_inc(gains_T, 1)
            for s in range(2):
                pe.wait_ge(lo_done, s + 1)
            for t in range(NT):
                pe.wait_ge(x_in[t], 16)

            def x_transposes(m):
                if m >= 3:
                    pe.wait_ge(h_lo_ok, m - 2)
                for t in range(NT):
                    last = pe.transpose(ps[4 + m % 3][:, t * P:(t + 1) * P], x_nat[:, t, m * P:(m + 1) * P], ident[:, :])
                last.then_inc(x_T, 1)
            x_transposes(0)
            x_transposes(1)
            for k in range(KD):
                if k + 2 < KD:
                    x_transposes(k + 2)
                pe.wait_ge(h_lo_ok, k + 1)
                for s in range(2):
                    last = three(ps[s][:, :], w_hi[s][:, k * P:(k + 1) * P], w_lo[s][:, k * P:(k + 1) * P],
                                 h_hi[:, k, :], h_lo[:, k, :], k == 0, k == KD - 1)
                    if k == KD - 1:
                        last.then_inc(unit_done, 1)
            pe.wait_ge(gains_ok, 1)
            statistic(N_X, Q_CQ)
            gemm(2, 0, [2], KD, h_hi, h_lo)
            gemm(3, 1, [3], KD, h_hi, h_lo, width=QK)

            def filler(u, g, b):
                pe.wait_ge(evac, g - 1)
                gemm(u, u % 2, [b], KD, h_hi, h_lo)

            pe.wait_ge(evac, 2)
            filler(4, 4, 0)
            pe.wait_ge(rs_ok, 1)
            statistic(N_CQ, Q_CKV)
            filler(5, 5, 1)
            pe.wait_ge(rs_ok, 2)
            statistic(N_CKV, Q_X2)
            pe.wait_ge(wu_lo_ok, 1)
            pe.wait_ge(c_lo_ok, 3)
            v_hi_w = wu_hi[:, 1536:2560].rearrange("p (h d) -> p h d", h=NH)[:, :, NOPE:NOPE + DV]
            v_lo_w = wu_lo[:, 1536:2560].rearrange("p (h d) -> p h d", h=NH)[:, :, NOPE:NOPE + DV]
            for t in range(NT):
                if t >= 2:
                    pe.wait_ge(va_lo_ok, t - 1)
                else:
                    pe.wait_ge(evac, 4)
                c = slice(t * P, (t + 1) * P)
                three(bank(2 + t % 2, NH), ckv_hi[:, c], ckv_lo[:, c], v_hi_w, v_lo_w, True, True).then_inc(va_mm, 1)

            def mla_proj(h):
                for k in range(2):
                    c = k * 768 + h * QK
                    last = three(ps[4][0:QK, :], wu_hi[:, c:c + QK], wu_lo[:, c:c + QK],
                                 cq_hi[:, k, :], cq_lo[:, k, :], k == 0, k == 1)
                last.then_inc(proj_mm, 1)
                c = 1536 + h * (NOPE + DV)
                three(ps[5][0:NOPE, :], wu_hi[:, c:c + NOPE], wu_lo[:, c:c + NOPE],
                      ckv_hi[:, :], ckv_lo[:, :], True, True).then_inc(proj_mm, 1)

            S_BANK = (2, 3, 7, 2)

            def mla_scores(h):
                pe.wait_ge(qk_lo_ok, 3 * h + 3)
                b = h % 2
                for i in range(NT):
                    n = max(256, (i + 1) * P)
                    if i == 3:
                        pe.wait_ge(s_ok, 4 * h + 1)
                    elif h >= 1:
                        pe.wait_ge(s_ok, 4 * h)
                    elif i == 2:
                        pe.wait_ge(rs_ok, 3)
                    else:
                        pe.wait_ge(va_lo_ok, NT)
                    c = slice(i * P, (i + 1) * P)
                    three(ps[S_BANK[i]][:, 0:n], q_hi[b][0:QK, c], q_lo[b][0:QK, c],
                          k_hi[b][0:QK, 0:n], k_lo[b][0:QK, 0:n], True, True).then_inc(s_mm, 1)

            def mla_transposes(h):
                pe.wait_ge(qk_lo_ok, min(3 * (h + 1) + 2, 3 * NH))
                for i in range(NT):
                    pe.wait_ge(p_ok, 4 * h + i + 1)
                    if i >= 2:
                        pe.wait_ge(pt_lo_ok, 4 * h + i - 1)
                    at = (0, 128, 384, 768)[i]
                    for j in range(i + 1):
                        last = pe.transpose(ps[4 + i % 2][:, j * P:(j + 1) * P], probs[:, at + j * P:at + (j + 1) * P], ident[:, :])
                    last.then_inc(t_mm, 1)

            def pv(dst, v_hi_t, v_lo_t, h, r_hi, r_lo):
                c = slice(h // 2 * P, h // 2 * P + P)
                for j in range(NT):
                    last = three(ps[dst][:, Q0[j]:S], v_hi_t[:, j, c], v_lo_t[:, j, c], r_hi(j), r_lo(j), j == 0, j == NT - 1)
                return last

            def mla_pv(h):
                pe.wait_ge(pt_lo_ok, 4 * h + 4)
                if h >= 1:
                    pe.wait_ge(o_ok, h)
                else:
                    pe.wait_ge(zero_ok, 2)
                pv(6, va_hi, va_lo, h, lambda j: pT[:, j * PT_STEP + Q0[j]:j * PT_STEP + S],
                   lambda j: pT[:, 1664 + j * PT_STEP + Q0[j]:1664 + j * PT_STEP + S]).then_inc(pv_mm, 1)

            pe.wait_ge(c_lo_ok, 3)
            mla_proj(0)
            for h in range(NH):
                mla_scores(h)
                if h >= 1:
                    mla_pv(h - 1)
                if h + 1 < NH:
                    if h >= 1:
                        pe.wait_ge(pt_lo_ok, 4 * h)
                    else:
                        pe.wait_ge(qk_lo_ok, 3)
                    mla_proj(h + 1)
                for u in fills[h][0]:
                    filler(u, u, u % 2)
                mla_transposes(h)
                for u in fills[h][1]:
                    filler(u, u, u % 2)
            filler(U_GATE, U_GATE, 0)
            mla_pv(NH - 1)

            pe.wait_ge(evac, G_GATE)
            for t in range(NT):
                if t >= 2:
                    pe.wait_ge(vb_lo_ok, t - 1)
                else:
                    pe.wait_ge(pt_lo_ok, 4 * NH)
                for j in range(4):
                    last = pe.transpose(ps[4 + t % 2][:, j * P:(j + 1) * P], sbvT[:, j, t * P:(t + 1) * P], ident[:, :])
                last.then_inc(vT_mm, 1)

            def sb_scores(h):
                pe.wait_ge(sq_stage_lo, h + h // 2 + 2)
                b = h % 2
                for n, j in enumerate((3, 2, 1, 0)):
                    if h >= 1:
                        pe.wait_ge(a_ok, 4 * (h - 1) + n + 1)
                    elif n == 0:
                        pe.wait_ge(vb_lo_ok, NT)
                    c = slice(j * P, (j + 1) * P)
                    kb = h // 2 % 2
                    acc = ps[2 + j][:, 0:S - Q0[j]]
                    q = slice(Q0[j], S)
                    three(acc, ks_hi[kb][:, c], ks_lo[kb][:, c], qs_hi[b][:, q], qs_lo[b][:, q], True, True).then_inc(z_mm, 1)

            def sb_suffix(h):
                for n, j in enumerate((3, 2, 1, 0)):
                    pe.wait_ge(sp_lo_ok, 4 * h + n + 1)
                    w = S - Q0[j]
                    for part in (sp_hi, sp_lo):
                        last = pe.matmul(ps[2 + j][:, 0:w], neg_tri[:, :], part[:, OFF[j]:OFF[j] + w],
                                         start=False, stop=True, skip_group_check=True)
                        for k in range(j + 1, NT):
                            last = pe.matmul(ps[2 + j][:, Q0[k] - Q0[j]:w], neg_ones[:, :],
                                             part[:, OFF[k]:OFF[k] + S - Q0[k]],
                                             start=False, stop=True, skip_group_check=True)
                    last.then_inc(w_mm, 1)

            def sb_pv(h):
                pe.wait_ge(a_lo_ok, 4 * h + 4)
                if h >= 1:
                    pe.wait_ge(ob_ok, h)
                else:
                    pe.wait_ge(o_ok, NH)
                pv(6, vb_hi, vb_lo, h, lambda j: a_hi[:, OFF[j]:OFF[j] + S - Q0[j]],
                   lambda j: a_lo[:, OFF[j]:OFF[j] + S - Q0[j]]).then_inc(pvb_mm, 1)

            pe.wait_ge(zero_ok, 3)
            for h in range(SBH):
                sb_scores(h)
                if h >= 1:
                    sb_pv(h - 1)
                u = U_GATE + 2 * h
                if h >= 1:
                    filler(u, u, 0)
                sb_suffix(h)
                filler(u + 1, u + 1, 1)

            pe.wait_ge(oa_lo_ok, 2)
            gemm(U_MERGE, 0, [0, 1], 4, oa_hi, oa_lo, free=lambda b: pe.wait_ge(evac, G_MERGE - 1 + b))
            sb_pv(SBH - 1)
            pe.wait_ge(ob_ok, SBH)
            gemm(U_MERGE + 1, 1, [2, 3], 4, ob_hi, ob_lo)

            def merge(t):
                pe.wait_ge(evac, G_MERGE + 4 * t - 2)
                gemm(U_MERGE + 2 * t, 0, [0, 1], 4, oa_hi, oa_lo)
                pe.wait_ge(evac, G_MERGE + 4 * t)
                gemm(U_MERGE + 2 * t + 1, 1, [2, 3], 4, ob_hi, ob_lo)
            repeat(pe, 1, 3, merge)

            def wo(i):
                for s in range(2):
                    pe.wait_ge(evac, G_WO - 1 + 2 * i + s)
                    gemm(U_WO + 2 * i + s, s, [s], KD, m_hi, m_lo)
            pe.wait_ge(evac, G_WO - 2)
            gemm(U_WO, 0, [0], KD, m_hi, m_lo, ready=lambda k: pe.wait_ge(m_lo_ok, k + 1))
            gemm(U_WO + 1, 1, [1], KD, m_hi, m_lo)
            pe.wait_ge(mem_n, 2)
            for m in range(KD):
                for t in range(2):
                    c = m % 2 * MEM + t * P
                    last = pe.transpose(ps[4 + m // 2][:, c:c + P], mem_nat[:, t, m * P:(m + 1) * P], ident[:, :])
                if m % 2:
                    last.then_inc(mem_T, 1)
            repeat(pe, 1, 3, wo)

            pe.wait_ge(mn_lo_ok, KD)
            for j in range(4):
                u, s = U_XV + j, j % 2
                pe.wait_ge(lo_done, u + 1)
                for k in range(2):
                    w = slice(k * S, (k + 1) * S)
                    for t in range(2):
                        c = slice(t * P, (t + 1) * P)
                        last = three(ps[4 + t][:, :], mn_hi[:, 2 * j + k, c], mn_lo[:, 2 * j + k, c],
                                     w_hi[s][:, w], w_lo[s][:, w], j == 0 and k == 0, j == 3 and k == 1)
                last.then_inc(unit_done, 1)
                if j == 1:
                    statistic(N_X2, Q_X3)

            def x_keys(h):
                pe.wait_ge(evac, G_XKQ + 2 * h - 1)
                gemm(U_XKQ + 2 * h, 0, [0], KD, mn_hi, mn_lo, n=MEM)

            def x_queries(h):
                pe.wait_ge(evac, G_XKQ + 2 * h)
                gemm(U_XKQ + 2 * h + 1, 1, [1], KD, h_hi, h_lo)

            def x_scores(h):
                pe.wait_ge(xq_lo_ok, h + 1)
                pe.wait_ge(evac, G_XKQ + 2 * h + 1)
                for i in range(NT):
                    if h >= 1 and i % 2 == 0:
                        pe.wait_ge(xe_ok, 4 * (h - 1) + i + 2)
                    c = slice(i * P, (i + 1) * P)
                    last = three(ps[2 + i // 2][:, i % 2 * MEM:(i % 2 + 1) * MEM], xq_hi[:, h, c], xq_lo[:, h, c],
                                 xk_hi[:, h, :], xk_lo[:, h, :], True, True)
                    if i % 2:
                        last.then_inc(xs_mm, 1)

            def x_transposes_of(h):
                for j in range(2):
                    pe.wait_ge(xp_ok, 4 * h + 4)
                    if h >= 1:
                        pe.wait_ge(xt_lo_ok, 2 * h - 1 + j)
                    else:
                        pe.wait_ge(xv_lo_ok, 2)
                    for i in range(NT):
                        last = pe.transpose(ps[4 + j][:, i * P:(i + 1) * P], xp[h % 2][:, i, j * P:(j + 1) * P], ident[:, :])
                    last.then_inc(xt_mm, 1)

            def x_pv(h):
                pe.wait_ge(xt_lo_ok, 2 * h + 2)
                if h >= 1:
                    pe.wait_ge(xo_lo_ok, h)
                c = slice(h * XD, (h + 1) * XD)
                for j in range(2):
                    last = three(ps[6][:, :], xv_hi[:, j, c], xv_lo[:, j, c], xpT_hi[:, j, :], xpT_lo[:, j, :], j == 0, j == 1)
                last.then_inc(xpv_mm, 1)

            def xo_part(v, heads):
                s = v % 2
                for b in range(2):
                    for k in heads:
                        pe.wait_ge(xo_lo_ok, k + 1)
                        c = (2 * k + b) * P
                        last = three(ps[2 * s + b][:, :], w_hi[s][:, c:c + P], w_lo[s][:, c:c + P],
                                     xo_hi[:, k, :], xo_lo[:, k, :], k == 0, k == XH - 1)
                    if heads[-1] == XH - 1:
                        last.then_inc((xo_mm, unit_done)[b], 1)

            pe.wait_ge(h_lo_ok, 2 * KD)
            x_keys(0)
            x_queries(0)
            x_keys(1)
            x_scores(0)
            x_queries(1)
            x_transposes_of(0)
            x_keys(2)
            x_pv(0)
            x_scores(1)
            x_queries(2)
            x_transposes_of(1)
            x_keys(3)
            x_pv(1)
            x_scores(2)
            x_queries(3)
            x_transposes_of(2)
            pe.wait_ge(lo_done, U_XO + 1)
            pe.wait_ge(evac, G_XO)
            xo_part(0, [0, 1])
            x_pv(2)
            x_scores(3)
            xo_part(0, [2])
            x_transposes_of(3)
            pe.wait_ge(lo_done, U_XO + 2)
            pe.wait_ge(xe_ok, 4 * XH)
            xo_part(1, [0, 1, 2])
            x_pv(3)
            xo_part(0, [3])
            xo_part(1, [3])
            for v in (2, 3):
                pe.wait_ge(lo_done, U_XO + v + 1)
                pe.wait_ge(evac, G_XO + 2 * v - 2)
                xo_part(v, [0, 1, 2, 3])

            def ffn(i):
                for b in range(2):
                    pe.wait_ge(evac, G_FFN - 2 + 4 * i + 2 * b)
                    gemm(U_FFN + 4 * i + 2 * b, 0, [2 * b], KD, h_hi, h_lo)
                    gemm(U_FFN + 4 * i + 2 * b + 1, 1, [2 * b + 1], KD, h_hi, h_lo)
            pe.wait_ge(evac, G_XO + 6)
            gemm(U_FFN, 0, [0], KD, h_hi, h_lo, ready=lambda k: pe.wait_ge(h_lo_ok, 2 * KD + k + 1))
            statistic(N_X3, Q_X4)
            gemm(U_FFN + 1, 1, [1], KD, h_hi, h_lo)
            pe.wait_ge(evac, G_FFN)
            gemm(U_FFN + 2, 0, [2], KD, h_hi, h_lo)
            gemm(U_FFN + 3, 1, [3], KD, h_hi, h_lo)
            repeat(pe, 1, KF // 2 - 1, ffn)

            def y_transposes(i, k):
                pe.wait_ge(y_ok, 8 * i + k + 1)
                for t in range(NT):
                    last = pe.transpose(ps[2 + t][:, k * P:(k + 1) * P], yT[:, k, t * P:(t + 1) * P], ident[:, :])
                if k == 3:
                    last.then_inc(yT_mm, 1)

            def down_half(i):
                for k in range(4):
                    pe.wait_ge(evac, G_DOWN - 1 + 4 * i + k)
                    for j in range(3):
                        pe.wait_ge(f_lo_ok, KF if j == 2 else 2 * DOWN_K[0])
                        gemm(U_DOWN + 12 * i + 3 * k + j, (3 * k + j) % 2, [k % 2], DOWN_K[j], f_hi, f_lo,
                             start=j == 0, stop=j == 2, k0=sum(DOWN_K[:j]))
                        if j == 0 and k >= 1:
                            y_transposes(i, k - 1)
                y_transposes(i, 3)
            repeat(pe, 0, 2, down_half)

            pe.wait_ge(sq_added, Q_X4 + KD - 1)
            pe.wait_ge(sq_ok, Q_X4 + KD)
            for t in range(NT):
                c = slice(t * P, (t + 1) * P)
                pe.matmul(ps[7][:, t:t + 1], sq_sum[:, c], ones[:, 0:1], start=True, stop=False)
                last = pe.matmul(ps[7][:, t:t + 1], sq_tile[:, c], ones[:, 0:1], start=False, stop=True)
            last.then_inc(stat_ok, 1)

        @block.scalar
        def _(act):
            steps = Steps(act, act_step)

            def exp_and_ln():
                act.preload_act_table_set("natural_log_exp_and_others")

            def split_hi(u, s, n=1024, first=False):
                act.wait_ge(raw_in[s], 8 * (u - s) + 16)
                if not first:
                    act.wait_ge(unit_done, u - 1)
                act.activation(w_hi[s][:, 0:n], raw[s][:, 0:n], ACT.Copy).then_inc(hi_done, 1)

            def square(n, src):
                if n > 0 if isinstance(n, int) else True:
                    act.wait_ge(sq_added, n)
                act.activation(sq_tile[:, :].rearrange("p (a n) -> p a n", a=1), src, ACT.Square).then_inc(sq_ok, 1)

            def inv_rms(n, dst, size):
                act.preload_act_table_set("natural_log")
                act.wait_ge(stat_ok, n + 1)
                act.activation(dst, ps[7][:, :], ACT.Ln, scale=1.0 / size, bias=eps_c).then_inc(ln_ok, 1)
                act.wait_ge(ln_ok, n + 1)
                exp_and_ln()
                act.activation(dst, dst, ACT.Exp, scale=-0.5).then_inc(rs_ok, 1)

            for t in range(NT):
                act.dma_start(x_nat[:, t, :], x[0, t * P:(t + 1) * P, :]).then_inc(x_in[t], 16)
            act.wait_ge(pool_const, 4)
            act.activation(neg_tri[:, :], scratch[:, :], ACT.Copy).then_inc(const_r, 1)
            act.activation(neg_ones[:, :], ones[:, :], ACT.Copy, scale=-1.0).then_inc(const_r, 1)
            split_hi(0, 0, first=True)
            split_hi(1, 1, first=True)
            act.wait_ge(trig_arg, 1)
            r = slice(NOPE, QK)
            act.activation(sin_t[r, :], ang[r, :], ACT.Sin).then_inc(trig_ok, 1)
            act.activation(cos_t[r, :], turns[r, :], ACT.Sin, bias=half_pi_c[r, :]).then_inc(trig_ok, 1)
            act.wait_ge(gains_ok, 1)

            def gained(dst, m, src, row, ok):
                act.activation(tile(dst, m), src, ACT.Copy, scale=col(gains, row + m)).then_inc(ok, 1)

            for m in range(KD):
                act.wait_ge(x_T, m + 1)
                act.wait_ge(x_kept, m + 1)
                square(Q_X + m, tile(xT, m))
                gained(h_hi, m, tile(xT, m), R_MIX, h_hi_ok)
            act.wait_ge(wu_in, 32)
            act.activation(wu_hi[:, :], wu_raw[:, :], ACT.Copy).then_inc(wu_hi_ok, 1)
            split_hi(2, 0)
            split_hi(3, 1, KD * QK)
            inv_rms(N_X, rs[:, :], D)
            split_hi(4, 0)
            for n in range(3):
                act.wait_ge(evac, n + 1)
                square(Q_CQ + n, tile(c_raw, n))
            inv_rms(N_CQ, rs_c[0][:, :], QR)
            split_hi(5, 1)
            for n in range(2):
                act.wait_ge(cn_ok, n + 1)
                act.activation(cq_hi[:, n, :], c_norm[:, :], ACT.Copy).then_inc(c_hi_ok, 1)
            inv_rms(N_CKV, rs_c[1][:, :], KVR)
            act.wait_ge(cn_ok, 3)
            act.activation(ckv_hi[:, :], c_norm[:, :], ACT.Copy).then_inc(c_hi_ok, 1)
            act.wait_ge(kr_ok, 1)
            for b in range(2):
                act.activation(k_hi[b][r, :], roped[r, :], ACT.Copy).then_inc(kr_hi_ok, 1)
            for t in range(NT):
                act.wait_ge(va_mm, t + 1)
                act.activation(va_hi[:, t, :], ps[2 + t % 2][:, :], ACT.Copy).then_inc(va_hi_ok, 1)
            split_hi(6, 0)

            def stage_hi(h):
                b = h % 2
                act.wait_ge(proj_mm, 2 * h + 1)
                if h >= 2:
                    act.wait_ge(s_mm, 4 * (h - 1))
                act.activation(q_hi[b][0:NOPE, :], ps[4][0:NOPE, :], ACT.Copy).then_inc(qk_hi_ok, 1)
                act.wait_ge(proj_mm, 2 * h + 2)
                act.activation(k_hi[b][0:NOPE, :], ps[5][0:NOPE, :], ACT.Copy).then_inc(qk_hi_ok, 1)
                act.wait_ge(rope_ok, h + 1)
                act.activation(q_hi[b][r, :], roped[r, :], ACT.Copy).then_inc(qk_hi_ok, 1)

            def mla_out(h):
                act.wait_ge(pv_mm, h + 1)
                rows = slice(h % 2 * DV, (h % 2 + 1) * DV)
                act.activation(oa[rows, h // 2, :], ps[6][rows, :], ACT.Copy).then_inc(o_ok, 1)

            stage_hi(0)
            for h in range(NH):
                for i in range(NT):
                    at, w = (0, 128, 384, 768)[i], (i + 1) * P
                    act.wait_ge(s_ok, 4 * h + i + 1)
                    act.activation(probs[:, at:at + w], probs[:, at:at + w], ACT.Exp, bias=stat[:, 4 + i:5 + i],
                                   scale=MLA_SCALE, accum_out=stat[:, 8 + i:9 + i]).then_inc(e_ok, 1)
                if h >= 1:
                    mla_out(h - 1)
                if h + 1 < NH:
                    stage_hi(h + 1)
                for u in fills[h][0]:
                    split_hi(u + 1, (u + 1) % 2)
                for i in range(NT):
                    act.wait_ge(t_mm, 4 * h + i + 1)
                    if h >= 1 and i == 0:
                        act.wait_ge(pv_mm, h)
                    if True:
                        dst = pT[:, i * P:i * P + (i + 1) * PT_STEP].rearrange("p (j c) -> p j c", c=PT_STEP)[:, :, 0:P]
                        act.activation(dst, bank(4 + i % 2, i + 1, (i + 1) * P), ACT.Copy).then_inc(pt_hi_ok, 1)
                for u in fills[h][1]:
                    split_hi(u + 1, (u + 1) % 2)
            split_hi(U_GATE + 1, 1)
            mla_out(NH - 1)

            for t in range(NT):
                act.wait_ge(vT_mm, t + 1)
                act.activation(vb_hi[:, t, :], ps[4 + t % 2][:, :], ACT.Copy).then_inc(vb_hi_ok, 1)

            def sb_stage_hi(h):
                rows = slice(h % 2 * SBD, (h % 2 + 1) * SBD)
                if h >= 2:
                    act.wait_ge(z_mm, 4 * (h - 1))
                if h % 2 == 0:
                    kb = h // 2 % 2
                    act.activation(ks_hi[kb][:, :], sbk[:, h // 2, :], ACT.Copy).then_inc(sq_stage_hi, 1)
                act.activation(qs_hi[h % 2][rows, :], sbq[rows, h // 2, :], ACT.Copy).then_inc(sq_stage_hi, 1)

            def sb_out(h):
                act.wait_ge(pvb_mm, h + 1)
                rows = slice(h % 2 * SBD, (h % 2 + 1) * SBD)
                act.activation(ob_hi[rows, h // 2, :], ps[6][rows, :], ACT.Copy).then_inc(ob_hi_ok, 1)

            S_AT = (0, 512, 896, 1152)

            sb_stage_hi(0)
            for h in range(SBH):
                for n, j in enumerate((3, 2, 1, 0)):
                    st = stick[:, S_AT[j]:S_AT[j] + S - j * P]
                    act.wait_ge(z_ok, 4 * h + n + 1)
                    if h >= 1:
                        act.wait_ge(a_lo_ok, 4 * (h - 1) + n + 1)
                    d0 = j * P - Q0[j]
                    steps.link(act.activation(st, ps[2 + j][:, d0:d0 + S - j * P], ACT.Abs))
                    steps.link(act.activation(st, st, ACT.Exp, scale=-1.0))
                    act.activation(st, st, ACT.Ln, bias=one_c).then_inc(l_ok, 1)
                for n, j in enumerate((3, 2, 1, 0)):
                    w = S - j * P
                    act.wait_ge(sp_ok, 4 * h + n + 1)
                    if h >= 1 and n == 0:
                        act.wait_ge(w_mm, 4 * h)
                    d = OFF[j] + j * P - Q0[j]
                    act.activation(sp_hi[:, d:d + w], stick[:, S_AT[j]:S_AT[j] + w], ACT.Copy).then_inc(sp_hi_ok, 1)
                if h >= 1:
                    sb_out(h - 1)
                if h >= 1:
                    u = U_GATE + 2 * h
                    split_hi(u + 1, (u + 1) % 2)
                if h + 1 < SBH:
                    sb_stage_hi(h + 1)
                if h >= SBH - 2:
                    act.wait_ge(sq_stage_lo, 11)
                    t = 2 * (h - SBH + 2)
                    act.activation(oa_hi[:, t:t + 2, :], oa[:, t:t + 2, :], ACT.Copy).then_inc(oa_hi_ok, 1)
                for n, j in enumerate((3, 2, 1, 0)):
                    w = S - j * P
                    act.wait_ge(w_mm, 4 * h + n + 1)
                    act.wait_ge(sp_lo_ok, 4 * h + n + 1)
                    d0 = j * P - Q0[j]
                    act.activation(stick[:, S_AT[j]:S_AT[j] + w], ps[2 + j][:, d0:d0 + w], ACT.Exp).then_inc(a_ok, 1)
                for n, j in enumerate((3, 2, 1, 0)):
                    w = S - j * P
                    act.wait_ge(a_ok, 4 * h + n + 1)
                    if h >= 1 and n == 0:
                        act.wait_ge(pvb_mm, h)
                    d = OFF[j] + j * P - Q0[j]
                    act.activation(a_hi[:, d:d + w], stick[:, S_AT[j]:S_AT[j] + w], ACT.Copy).then_inc(a_hi_ok, 1)
                u = U_GATE + 2 * h + 1
                split_hi(u + 1, (u + 1) % 2)
            split_hi(U_MERGE + 1, 1)
            act.wait_ge(mem_in, 16)
            for t in range(2):
                if t:
                    act.wait_ge(mem_sq, 1)
                act.activation(mem_junk[:, :], mem_nat[:, t, :], ACT.Square, accum_out=stat_x[:, 4 + t:5 + t]).then_inc(mem_sq, 1)
            sb_out(SBH - 1)
            act.wait_ge(evac, G_MERGE)

            def merge(t, first=False):
                if not first:
                    split_hi(U_MERGE + 2 * t + 1, 1)
                for part in range(2):
                    for b in range(2):
                        g = tile(gates, 8 * part + 2 * t + b)
                        act.activation(g, g, ACT.Sigmoid, bias=col(gains, R_BIAS + 8 * part + 2 * t + b)).then_inc(sig_ok, 1)
                split_hi(U_MERGE + 2 * t + 2, 0)
                for b in range(2):
                    act.wait_ge(m_ok, 2 * t + b + 1)
                    act.activation(tile(m_hi, 2 * t + b), tile(gates, 2 * t + b), ACT.Copy).then_inc(m_hi_ok, 1)
            merge(0, first=True)
            repeat(act, 1, 3, merge)

            split_hi(U_WO + 1, 1)
            act.preload_act_table_set("natural_log")
            act.wait_ge(mem_sq, 2)
            steps.link(act.activation(stat_x[:, 4:6], stat_x[:, 4:6], ACT.Ln, scale=1.0 / D, bias=eps_c))
            exp_and_ln()
            act.activation(stat_x[:, 4:6], stat_x[:, 4:6], ACT.Exp, scale=-0.5).then_inc(mem_rs, 1)

            def wo(i, first=False):
                for s in range(2):
                    m = 2 * i + s
                    if not (first and s == 0):
                        split_hi(U_WO + m + 1, (s + 1) % 2)
                    act.wait_ge(evac, G_WO + m + 1)
                    square(Q_X2 + m, tile(xT, m))
                    gained(h_hi, m, tile(xT, m), R_X, h_hi_ok)
            wo(0, first=True)
            for m in range(KD):
                act.wait_ge(mem_T, m // 2 + 1)
                act.activation(mn_hi[:, m, :], ps[4 + m // 2][:, m % 2 * MEM:(m % 2 + 1) * MEM], ACT.Copy,
                               scale=gains[:, R_MEM + m:R_MEM + m + 1]).then_inc(mn_hi_ok, 1)
            repeat(act, 1, 3, wo)

            for u in (U_XV + 1, U_XV + 2, U_XV + 3):
                split_hi(u, u % 2)
            inv_rms(N_X2, rs[:, :], D)
            split_hi(U_XKQ, 0)
            act.wait_ge(unit_done, U_XKQ)
            for t in range(2):
                act.activation(xv_hi[:, t, :], ps[4 + t][:, :], ACT.Copy).then_inc(xv_hi_ok, 1)

            def x_keys(h):
                split_hi(U_XKQ + 2 * h + 1, 1)
                act.wait_ge(unit_done, U_XKQ + 2 * h + 1)
                act.activation(xk_hi[:, h, :], ps[0][:, 0:MEM], ACT.Copy).then_inc(xk_hi_ok, 1)

            def x_queries(h):
                split_hi(U_XKQ + 2 * h + 2, 0)
                act.wait_ge(evac, G_XKQ + 2 * h + 2)
                act.activation(xq_hi[:, h, :], xq_raw[h % 2][:, :], ACT.Copy).then_inc(xq_hi_ok, 1)

            def x_exp(h):
                if h >= 1:
                    act.wait_ge(xp_ok, 4 * h)
                for i in range(NT):
                    act.wait_ge(xs_max, 2 * h + i // 2 + 1)
                    act.activation(xp[h % 2][:, i, :], ps[2 + i // 2][:, i % 2 * MEM:(i % 2 + 1) * MEM], ACT.Exp,
                                   bias=stat_x[:, 8 + i:9 + i], scale=X_SCALE,
                                   accum_out=stat_x[:, 12 + i:13 + i]).then_inc(xe_ok, 1)

            def x_turned(h):
                for j in range(2):
                    act.wait_ge(xt_mm, 2 * h + j + 1)
                    if h >= 1:
                        act.wait_ge(xpv_mm, h)
                    act.activation(xpT_hi[:, j, :], ps[4 + j][:, :], ACT.Copy).then_inc(xt_hi_ok, 1)

            def x_out(h):
                act.wait_ge(xpv_mm, h + 1)
                act.activation(xo_hi[:, h, :], ps[6][:, :], ACT.Copy).then_inc(xo_hi_ok, 1)

            x_keys(0)
            x_queries(0)
            x_keys(1)
            for h in range(XH):
                x_exp(h)
                if h + 1 < XH:
                    x_queries(h + 1)
                x_turned(h)
                if h + 2 < XH:
                    x_keys(h + 2)
                elif h + 2 == XH:
                    split_hi(U_XO + 1, 1)
                x_out(h)

            for v in range(4):
                if v >= 1:
                    split_hi(U_XO + v + 1, (v + 1) % 2)
                for b in range(2):
                    m = 2 * v + b
                    act.wait_ge(evac, G_XO + m + 1)
                    gained(h_hi, m, tile(xT, m), R_FFN, h_hi_ok)
                    square(Q_X3 + m, tile(xT, m))

            split_hi(U_FFN + 1, 1)
            inv_rms(N_X3, rs[:, :], D)

            def ffn(i, head=False):
                for b in range(2):
                    m = 2 * i + b
                    if not (head and b == 0):
                        split_hi(U_FFN + 2 * m + 1, 1)
                    split_hi(U_FFN + 2 * m + 2, 0)
                    act.wait_ge(evac, G_FFN + 2 * m + 1)
                    act.activation(g_t[b][:, :], g_t[b][:, :], ACT.Silu).then_inc(silu_ok, 1)
                    act.wait_ge(f_ok, m + 1)
                    act.activation(tile(f_hi, m), u_t[b][:, :].rearrange("p (a n) -> p a n", a=1), ACT.Copy).then_inc(f_hi_ok, 1)
            ffn(0, head=True)
            repeat(act, 1, KF // 2 - 1, ffn)

            for i in range(2):
                for k in range(4):
                    for j in range(3):
                        c = 3 * k + j + 1
                        if c < 12 or i == 0:
                            split_hi(U_DOWN + 12 * i + c, c % 2, P * DOWN_K[c % 3])
                    m = 4 * i + k
                    act.wait_ge(evac, G_DOWN + m + 1)
                    square(Q_X4 + m, tile(xT, m))
                    act.activation(yT[:, k, :], xT[:, m, :], ACT.Copy, scale=gains[:, R_FINAL + m:R_FINAL + m + 1]).then_inc(y_ok, 1)
                if i == 0:
                    act.wait_ge(yT_mm, 1)
                    for t in range(NT):
                        act.activation(y_nat[:, t, 0:S], ps[2 + t][:, :], ACT.Copy).then_inc(y_ok, 1)
            act.preload_act_table_set("sqrt_and_others")
            act.wait_ge(stat_ok, N_X4 + 1)
            act.activation(stat[:, 0:4], ps[7][:, 0:4], ACT.Sqrt, scale=1.0 / D, bias=eps_c).then_inc(rs_ok, 1)
            act.wait_ge(y_rs, 1)
            act.wait_ge(yT_mm, 2)
            for t in range(NT):
                act.activation(y_nat[:, t, S:D], ps[2 + t][:, :], ACT.Copy, scale=stat[:, 4 + t:5 + t]).then_inc(y_right, 1)

        @block.gpsimd
        def _(pool):
            steps = Steps(pool, pool_step)
            steps.link(pool.memset(ident[:, :], 0.0))
            pool.affine_select(out=ident[:, :], in_=ident[:, :], compare_op=ALU.not_equal, fill=1.0, base=0,
                               pattern=[[-1, P]], channel_multiplier=1).then_inc(pool_const, 1)
            rows = ((g_mix[0], R_MIX, 8), (g_x[0], R_X, 8), (g_mem[0], R_MEM, 8), (g_ffn[0], R_FFN, 8),
                    (g_final, R_FINAL, 8), (b_gate[0].rearrange("a n -> (a n)"), R_BIAS, 16),
                    (g_q_lat[0], R_Q, 2), (g_kv_lat[0], R_KV, 1))
            for src, row, n in rows:
                pool.dma_start(gain_rows[row:row + n, :], src.rearrange("(k p) -> k p", p=P)).then_inc(gains_in, 16)
            pool.dma_start(pos_i[NOPE:QK, :], positions[0:1, :].to_broadcast([ROPE, S])).then_inc(pos_in, 16)
            pool.dma_start(consts[NOPE:QK, 3:4], signed_freq).then_inc(freq_in, 16)
            pool.dma_start(wu_raw[:, 0:1536].rearrange("p (k n) -> p k n", k=2),
                           w_uq[0].rearrange("(k p) n -> p k n", p=P)).then_inc(wu_in, 16)
            pool.dma_start(wu_raw[:, 1536:2560], w_ukv[0]).then_inc(wu_in, 16)
            pool.memset(ones[:, :], 1.0).then_inc(pool_const, 1)
            steps.link(pool.memset(scratch[:, :], -1.0))
            pool.affine_select(out=scratch[:, :], in_=scratch[:, :], compare_op=ALU.is_ge, fill=0.0, base=0,
                               pattern=[[-1, P]], channel_multiplier=1).then_inc(pool_const, 1)
            pool.memset(consts[:, 0:1], EPS)
            pool.memset(consts[:, 1:2], HALF_PI)
            pool.memset(consts[:, 2:3], 1.0).then_inc(pool_const, 1)
            pool.memset(mask_row[:, 0:384], 0.0)
            steps.link(pool.memset(mask_row[:, 384:512], 0.0))
            pool.affine_select(out=mask_row[:, 384:512], in_=mask_row[:, 384:512], compare_op=ALU.is_ge, fill=NEG,
                               base=0, pattern=[[-1, P]], channel_multiplier=1).then_inc(pool_const, 1)
            steps.link(pool.memset(mask_kq[:, :], 0.0))
            pool.affine_select(out=mask_kq[:, :], in_=mask_kq[:, :], compare_op=ALU.is_gt, fill=NEG,
                               base=0, pattern=[[1, P]], channel_multiplier=-1).then_inc(pool_const, 1)
            pool.memset(sq_sum[:, :], 0.0).then_inc(sum_clear, 1)

            added = [0]

            def add_squares(count, n_stat, loop=False):
                pool.wait_ge(sum_clear, n_stat + 1)
                q0 = added[0]

                def one(m):
                    pool.wait_ge(sq_ok, q0 + m + 1)
                    if q0 or not isinstance(m, int) or m:
                        pool.wait_ge(sq_added, q0 + m)
                    pool.tensor_tensor(sq_sum[:, :], sq_sum[:, :], sq_tile[:, :], ALU.add).then_inc(sq_added, 1)
                if loop:
                    repeat(pool, 0, count, one)
                else:
                    for m in range(count):
                        one(m)
                added[0] += count
                if n_stat < N_X4:
                    pool.wait_ge(stat_ok, n_stat + 1)
                    pool.memset(sq_sum[:, :], 0.0).then_inc(sum_clear, 1)

            add_squares(8, N_X)
            add_squares(2, N_CQ)
            add_squares(1, N_CKV)
            for h in range(NH):
                pool.wait_ge(dve_rope, 2 * h + 2)
                pool.wait_ge(rope_ok, h) if h else pool.wait_ge(sum_clear, 4)
                r = slice(NOPE, QK)
                steps.link(pool.tensor_tensor(swapped[r, :], swapped[r, :], sin_t[r, :], ALU.mult))
                pool.tensor_tensor(roped[r, :], roped[r, :], swapped[r, :], ALU.add).then_inc(rope_ok, 1)
            pool.wait_ge(z_mm, 4 * SBH)
            pool.dma_start(mem_nat[:, :, :], mem[0].rearrange("(t p) d -> p t d", p=P)).then_inc(mem_in, 16)
            pool.wait_ge(rope_ok, NH)
            add_squares(8, N_X2, loop=True)
            add_squares(8, N_X3, loop=True)
            add_squares(KD - 1, N_X4, loop=True)

        @block.vector
        def _(dve):
            steps = Steps(dve, dve_step)

            def split_lo(u, s, n=1024):
                dve.wait_ge(hi_done, u + 1)
                dve.tensor_tensor(w_lo[s][:, 0:n], raw[s][:, 0:n], fl(w_hi[s][:, 0:n]), ALU.subtract).then_inc(lo_done, 1)

            def gained_lo(m, row, count):
                dve.wait_ge(h_hi_ok, count)
                dve.scalar_tensor_tensor(out=tile(h_lo, m), in0=tile(xT, m), scalar=col(gains, row + m),
                                         in1=fl(tile(h_hi, m)), op0=ALU.mult, op1=ALU.subtract).then_inc(h_lo_ok, 1)

            r = slice(NOPE, QK)
            dve.wait_ge(gains_T, 1)
            dve.tensor_copy(gains[:, 0:R_ALL], ps[7][:, 0:R_ALL]).then_inc(gains_ok, 1)
            c1, c2 = 6.28125, 0.0019350051879882812
            c3 = float(2 * np.pi - c1 - c2)
            magic = 1.5 * 2.0 ** 23
            dve.wait_ge(pos_in, 16)
            dve.wait_ge(freq_in, 16)
            steps.link(dve.tensor_copy(turns[r, :], pos_i[r, :]))
            steps.link(dve.tensor_scalar(ang[r, :], turns[r, :], consts[r, 3:4], None, ALU.mult))
            for unit in (4096.0, 1.0):
                steps.link(dve.tensor_scalar(turns[r, :], ang[r, :], 1.0 / (2 * np.pi * unit), magic, ALU.mult, ALU.add))
                steps.link(dve.tensor_scalar(turns[r, :], turns[r, :], magic, unit, ALU.subtract, ALU.mult))
                for c in (c1, c2, c3):
                    steps.link(dve.scalar_tensor_tensor(out=ang[r, :], in0=turns[r, :], scalar=-c, in1=ang[r, :],
                                                        op0=ALU.mult, op1=ALU.add))
            pi32 = 3.1415925
            steps.link(dve.tensor_scalar(ang[r, :], ang[r, :], pi32, -pi32, ALU.min, ALU.max))
            dve.scalar_tensor_tensor(out=turns[r, :], in0=ang[r, :], scalar=-1.0, in1=ang[r, :], op0=ALU.mult,
                                     op1=ALU.min).then_inc(trig_arg, 1)
            split_lo(0, 0)
            split_lo(1, 1)
            for m in range(KD):
                dve.wait_ge(x_T, m + 1)
                dve.tensor_copy(tile(xT, m), bank(4 + m % 3)).then_inc(x_kept, 1)
                dve.wait_ge(x_kept, m + 1)
                gained_lo(m, R_MIX, m + 1)
            dve.wait_ge(wu_hi_ok, 1)
            dve.tensor_tensor(wu_lo[:, :], wu_raw[:, :], fl(wu_hi[:, :]), ALU.subtract).then_inc(wu_lo_ok, 1)
            split_lo(2, 0)
            dve.wait_ge(rs_ok, 1)
            for n in range(3):
                if n == 1:
                    split_lo(3, 1, KD * QK)
                if n == 2:
                    split_lo(4, 0)
                dve.wait_ge(unit_done, n + 1)
                dve.tensor_tensor(c_raw[:, n, :], ps[n][:, :], rs[:, :], ALU.mult).then_inc(evac, 1)
            dve.wait_ge(unit_done, 4)
            dve.tensor_tensor(c_raw[r, 3, :], ps[3][r, :], rs[r, :], ALU.mult).then_inc(evac, 1)
            dve.wait_ge(evac, 4)
            dve.wait_ge(trig_ok, 2)
            swap = list(range(ROPE // 2, ROPE)) + list(range(ROPE // 2))
            steps.link(dve.stream_shuffle(swapped[r, :], c_raw[r, 3, :], swap))
            steps.link(dve.tensor_tensor(swapped[r, :], swapped[r, :], sin_t[r, :], ALU.mult))
            steps.link(dve.tensor_tensor(roped[r, :], c_raw[r, 3, :], cos_t[r, :], ALU.mult))
            dve.tensor_tensor(roped[r, :], roped[r, :], swapped[r, :], ALU.add).then_inc(kr_ok, 1)

            def latent(n, row, dst_lo, src_hi, which):
                if n:
                    dve.wait_ge(c_hi_ok, n)
                dve.scalar_tensor_tensor(out=c_norm[:, :], in0=c_raw[:, n, :], scalar=gains[:, row:row + 1],
                                         in1=rs_c[which][:, :], op0=ALU.mult, op1=ALU.mult).then_inc(cn_ok, 1)
                dve.wait_ge(c_hi_ok, n + 1)
                dve.tensor_tensor(dst_lo, c_norm[:, :], fl(src_hi), ALU.subtract).then_inc(c_lo_ok, 1)
                dve.wait_ge(c_lo_ok, n + 1)

            def sb_epilogue(u):
                n = u - U_SB
                dve.wait_ge(unit_done, u + 1)
                dst = (sbq, sbk, sbvT)[n // 4][:, n % 4, :]
                dve.scalar_tensor_tensor(out=dst, in0=ps[u % 2][:, :], scalar=SB_SCALE if n < 4 else 1.0,
                                         in1=rs[:, :], op0=ALU.mult, op1=ALU.mult).then_inc(evac, 1)

            def gate_epilogue(u):
                dve.wait_ge(unit_done, u + 1)
                dve.tensor_tensor(gates[:, u - U_GATE, :], ps[u % 2][:, :], rs[:, :], ALU.mult).then_inc(evac, 1)

            dve.wait_ge(rs_ok, 2)
            split_lo(5, 1)
            for n in range(2):
                latent(n, R_Q + n, cq_lo[:, n, :], cq_hi[:, n, :], 0)
            dve.wait_ge(rs_ok, 3)
            latent(2, R_KV, ckv_lo[:, :], ckv_hi[:, :], 1)
            for b in range(2):
                dve.wait_ge(kr_hi_ok, b + 1)
                dve.tensor_tensor(k_lo[b][r, :], roped[r, :], fl(k_hi[b][r, :]), ALU.subtract).then_inc(kr_lo_ok, 1)
            sb_epilogue(4)
            for t in range(NT):
                dve.wait_ge(va_hi_ok, t + 1)
                dve.tensor_tensor(va_lo[:, t, :], ps[2 + t % 2][:, :], fl(va_hi[:, t, :]), ALU.subtract).then_inc(va_lo_ok, 1)
            sb_epilogue(5)
            split_lo(6, 0)
            dve.memset(pT[:, 3 * PT_STEP + 256:3 * PT_STEP + 384].bitcast(mybir.dt.uint32), 0).then_inc(zero_ok, 1)
            dve.memset(pT[:, 1664 + 3 * PT_STEP + 256:1664 + 3 * PT_STEP + 384].bitcast(mybir.dt.uint32), 0).then_inc(zero_ok, 1)

            def stage_lo(h):
                b = h % 2
                dve.wait_ge(proj_mm, 2 * h + 1)
                if h >= 1:
                    dve.wait_ge(qk_hi_ok, 3 * h)
                    dve.wait_ge(qk_lo_ok, 3 * h)
                else:
                    dve.wait_ge(kr_lo_ok, 2)
                dve.wait_ge(qk_hi_ok, 3 * h + 1)
                dve.stream_shuffle(swapped[r, :], ps[4][r, :], swap).then_inc(dve_rope, 1)
                dve.tensor_tensor(roped[r, :], ps[4][r, :], cos_t[r, :], ALU.mult).then_inc(dve_rope, 1)
                dve.tensor_tensor(q_lo[b][0:NOPE, :], ps[4][0:NOPE, :], fl(q_hi[b][0:NOPE, :]), ALU.subtract).then_inc(qk_lo_ok, 1)
                dve.wait_ge(qk_hi_ok, 3 * h + 2)
                dve.tensor_tensor(k_lo[b][0:NOPE, :], ps[5][0:NOPE, :], fl(k_hi[b][0:NOPE, :]), ALU.subtract).then_inc(qk_lo_ok, 1)

            def stage_rope_lo(h):
                b = h % 2
                dve.wait_ge(qk_hi_ok, 3 * h + 3)
                dve.tensor_tensor(q_lo[b][r, :], roped[r, :], fl(q_hi[b][r, :]), ALU.subtract).then_inc(qk_lo_ok, 1)

            dve.wait_ge(pool_const, 6)
            stage_lo(0)
            stage_rope_lo(0)
            S_BANK = (2, 3, 7, 2)
            for h in range(NH):
                for i in range(NT):
                    at, w = (0, 128, 384, 768)[i], (i + 1) * P
                    dve.wait_ge(s_mm, 4 * h + i + 1)
                    if h >= 1 and i == 0:
                        dve.wait_ge(t_mm, 4 * h)
                    steps.link(dve.tensor_tensor_reduce(out=probs[:, at:at + w], in0=ps[S_BANK[i]][:, 0:w],
                                                        in1=mask_row[:, S - w:S], scale=1.0, scalar=-3.0e38,
                                                        op0=ALU.add, op1=ALU.max, accum_out=stat[:, i:i + 1]))
                    dve.tensor_scalar(stat[:, 4 + i:5 + i], stat[:, i:i + 1], -MLA_SCALE, None, ALU.mult).then_inc(s_ok, 1)
                if h + 1 < NH:
                    stage_lo(h + 1)
                dve.wait_ge(e_ok, 4 * h + 4)
                steps.link(dve.reciprocal(stat[:, 12:16], stat[:, 8:12]))
                for i in range(NT):
                    at, w = (0, 128, 384, 768)[i], (i + 1) * P
                    dve.tensor_scalar(probs[:, at:at + w], probs[:, at:at + w], stat[:, 12 + i:13 + i], None, ALU.mult).then_inc(p_ok, 1)
                if h + 1 < NH:
                    stage_rope_lo(h + 1)
                for u in fills[h][0]:
                    split_lo(u + 1, (u + 1) % 2)
                    sb_epilogue(u)
                for i in range(NT):
                    dve.wait_ge(pt_hi_ok, 4 * h + i + 1)
                    v = slice(i * P, i * P + (i + 1) * PT_STEP)
                    hi = pT[:, v].rearrange("p (j c) -> p j c", c=PT_STEP)[:, :, 0:P]
                    lo = pT[:, 1664 + v.start:1664 + v.stop].rearrange("p (j c) -> p j c", c=PT_STEP)[:, :, 0:P]
                    dve.tensor_tensor(lo, bank(4 + i % 2, i + 1, (i + 1) * P), fl(hi), ALU.subtract).then_inc(pt_lo_ok, 1)
                for u in fills[h][1]:
                    split_lo(u + 1, (u + 1) % 2)
                    sb_epilogue(u)
            split_lo(U_GATE + 1, 1)
            dve.wait_ge(o_ok, NH)
            gate_epilogue(U_GATE)
            for t in range(NT):
                dve.wait_ge(vb_hi_ok, t + 1)
                dve.tensor_tensor(vb_lo[:, t, :], ps[4 + t % 2][:, :], fl(vb_hi[:, t, :]), ALU.subtract).then_inc(vb_lo_ok, 1)
            for part, base in ((sp_hi, 0), (sp_lo, 0), (a_hi, 0), (a_lo, 0)):
                z = part[:, OFF[3]:OFF[3] + P].bitcast(mybir.dt.uint32)
                last = dve.memset(z, 0)
            for b in range(2):
                rows = slice((1 - b) * SBD, (2 - b) * SBD)
                dve.memset(qs_hi[b][rows, :].bitcast(mybir.dt.uint32), 0)
                last = dve.memset(qs_lo[b][rows, :].bitcast(mybir.dt.uint32), 0)
            last.then_inc(zero_ok, 1)

            def sb_stage_lo(h):
                rows = slice(h % 2 * SBD, (h % 2 + 1) * SBD)
                n = h + (h + 1) // 2
                if h % 2 == 0:
                    kb = h // 2 % 2
                    n += 1
                    dve.wait_ge(sq_stage_hi, n)
                    dve.tensor_tensor(ks_lo[kb][:, :], sbk[:, h // 2, :], fl(ks_hi[kb][:, :]), ALU.subtract).then_inc(sq_stage_lo, 1)
                dve.wait_ge(sq_stage_hi, n + 1)
                dve.tensor_tensor(qs_lo[h % 2][rows, :], sbq[rows, h // 2, :], fl(qs_hi[h % 2][rows, :]), ALU.subtract).then_inc(sq_stage_lo, 1)

            def sb_out_lo(h):
                rows = slice(h % 2 * SBD, (h % 2 + 1) * SBD)
                dve.wait_ge(ob_hi_ok, h + 1)
                dve.tensor_tensor(ob_lo[rows, h // 2, :], ps[6][rows, :], fl(ob_hi[rows, h // 2, :]), ALU.subtract).then_inc(ob_ok, 1)

            S_AT = (0, 512, 896, 1152)
            sb_stage_lo(0)
            for h in range(SBH):
                for n, j in enumerate((3, 2, 1, 0)):
                    w, d0 = S - j * P, j * P - Q0[j]
                    dve.wait_ge(z_mm, 4 * h + n + 1)
                    dve.tensor_tensor(ps[2 + j][:, d0:d0 + P], ps[2 + j][:, d0:d0 + P], mask_kq[:, :], ALU.add).then_inc(z_ok, 1)
                for n, j in enumerate((3, 2, 1, 0)):
                    w, d0 = S - j * P, j * P - Q0[j]
                    st = stick[:, S_AT[j]:S_AT[j] + w]
                    dve.wait_ge(l_ok, 4 * h + n + 1)
                    dve.scalar_tensor_tensor(out=st, in0=ps[2 + j][:, d0:d0 + w], scalar=0.0, in1=st,
                                             op0=ALU.max, op1=ALU.add).then_inc(sp_ok, 1)
                for n, j in enumerate((3, 2, 1, 0)):
                    w = S - j * P
                    d = OFF[j] + j * P - Q0[j]
                    dve.wait_ge(sp_hi_ok, 4 * h + n + 1)
                    dve.tensor_tensor(sp_lo[:, d:d + w], stick[:, S_AT[j]:S_AT[j] + w], fl(sp_hi[:, d:d + w]), ALU.subtract).then_inc(sp_lo_ok, 1)
                if h >= 1:
                    sb_out_lo(h - 1)
                    u = U_GATE + 2 * h
                    split_lo(u + 1, (u + 1) % 2)
                    gate_epilogue(u)
                if h + 1 < SBH:
                    sb_stage_lo(h + 1)
                if h >= SBH - 2:
                    t = 2 * (h - SBH + 2)
                    dve.wait_ge(oa_hi_ok, h - SBH + 3)
                    dve.tensor_tensor(oa_lo[:, t:t + 2, :], oa[:, t:t + 2, :], fl(oa_hi[:, t:t + 2, :]), ALU.subtract).then_inc(oa_lo_ok, 1)
                for n, j in enumerate((3, 2, 1, 0)):
                    w = S - j * P
                    d = OFF[j] + j * P - Q0[j]
                    dve.wait_ge(a_hi_ok, 4 * h + n + 1)
                    dve.tensor_tensor(a_lo[:, d:d + w], stick[:, S_AT[j]:S_AT[j] + w], fl(a_hi[:, d:d + w]), ALU.subtract).then_inc(a_lo_ok, 1)
                u = U_GATE + 2 * h + 1
                split_lo(u + 1, (u + 1) % 2)
                gate_epilogue(u)
            split_lo(U_MERGE + 1, 1)
            sb_out_lo(SBH - 1)

            def merge(t, first=False):
                if not first:
                    split_lo(U_MERGE + 2 * t + 1, 1)
                for part in range(2):
                    if part == 1:
                        split_lo(U_MERGE + 2 * t + 2, 0)
                    dve.wait_ge(unit_done, U_MERGE + 2 * t + 1 + part)
                    dve.wait_ge(sig_ok, 4 * t + 2 + 2 * part)
                    for b in range(2):
                        g = tile(gates, 8 * part + 2 * t + b)
                        dve.tensor_tensor(g, bank(2 * part + b), g, ALU.mult).then_inc(evac, 1)
                for b in range(2):
                    dve.wait_ge(evac, G_MERGE + 4 * t + 3 + b)
                    dve.tensor_tensor(tile(gates, 2 * t + b), tile(gates, 2 * t + b), tile(gates, 8 + 2 * t + b), ALU.add).then_inc(m_ok, 1)
                for b in range(2):
                    dve.wait_ge(m_hi_ok, 2 * t + b + 1)
                    dve.tensor_tensor(tile(m_lo, 2 * t + b), tile(gates, 2 * t + b), fl(tile(m_hi, 2 * t + b)), ALU.subtract).then_inc(m_lo_ok, 1)
            merge(0, first=True)
            repeat(dve, 1, 3, merge)

            def residual(m, b):
                dve.tensor_tensor(tile(xT, m), bank(b), tile(xT, m), ALU.add).then_inc(evac, 1)

            split_lo(U_WO + 1, 1)
            dve.wait_ge(mem_rs, 1)
            for t in range(2):
                dve.tensor_scalar(mem_nat[:, t, :], mem_nat[:, t, :], stat_x[:, 4 + t:5 + t], None, ALU.mult).then_inc(mem_n, 1)

            def wo(i, first=False):
                for s in range(2):
                    m = 2 * i + s
                    if not (first and s == 0):
                        split_lo(U_WO + m + 1, (s + 1) % 2)
                    dve.wait_ge(unit_done, U_WO + m + 1)
                    residual(m, s)
                    gained_lo(m, R_X, KD + m + 1)
            wo(0, first=True)
            for m in range(KD):
                dve.wait_ge(mn_hi_ok, m // 2 * 2 + 2)
                dve.scalar_tensor_tensor(out=mn_lo[:, m, :], in0=ps[4 + m // 2][:, m % 2 * MEM:(m % 2 + 1) * MEM],
                                         scalar=gains[:, R_MEM + m:R_MEM + m + 1],
                                         in1=fl(mn_hi[:, m, :]), op0=ALU.mult, op1=ALU.subtract).then_inc(mn_lo_ok, 1)
            repeat(dve, 1, 3, wo)

            for u in (U_XV + 1, U_XV + 2, U_XV + 3, U_XKQ):
                split_lo(u, u % 2)
            for t in range(2):
                dve.wait_ge(xv_hi_ok, t + 1)
                dve.tensor_tensor(xv_lo[:, t, :], ps[4 + t][:, :], fl(xv_hi[:, t, :]), ALU.subtract).then_inc(xv_lo_ok, 1)
            dve.wait_ge(rs_ok, N_X2 + 1)

            def x_keys(h):
                split_lo(U_XKQ + 2 * h + 1, 1)
                dve.wait_ge(xk_hi_ok, h + 1)
                dve.tensor_tensor(xk_lo[:, h, :], ps[0][:, 0:MEM], fl(xk_hi[:, h, :]), ALU.subtract).then_inc(evac, 1)

            def x_queries(h):
                dve.wait_ge(unit_done, U_XKQ + 2 * h + 2)
                dve.tensor_tensor(xq_raw[h % 2][:, :], ps[1][:, :], rs[:, :], ALU.mult).then_inc(evac, 1)
                dve.wait_ge(xq_hi_ok, h + 1)
                dve.tensor_tensor(xq_lo[:, h, :], xq_raw[h % 2][:, :], fl(xq_hi[:, h, :]), ALU.subtract).then_inc(xq_lo_ok, 1)

            def x_softmax(h):
                for c in range(2):
                    dve.wait_ge(xs_mm, 2 * h + c + 1)
                    if h >= 1 and c == 0:
                        dve.wait_ge(xe_ok, 4 * h)
                    steps.link(dve.reduce_max(stat_x[:, 4 + 2 * c:6 + 2 * c], bank(2 + c, 2), AX_X))
                    dve.tensor_scalar(stat_x[:, 8 + 2 * c:10 + 2 * c], stat_x[:, 4 + 2 * c:6 + 2 * c], -X_SCALE, None, ALU.mult).then_inc(xs_max, 1)
                if h + 1 < XH:
                    split_lo(U_XKQ + 2 * h + 4, 0)
                dve.wait_ge(xe_ok, 4 * h + 4)
                steps.link(dve.reciprocal(stat_x[:, 16:20], stat_x[:, 12:16]))
                for i in range(NT):
                    dve.tensor_scalar(xp[h % 2][:, i, :], xp[h % 2][:, i, :], stat_x[:, 16 + i:17 + i], None, ALU.mult).then_inc(xp_ok, 1)

            x_keys(0)
            split_lo(U_XKQ + 2, 0)
            x_queries(0)
            x_keys(1)
            for h in range(XH):
                x_softmax(h)
                if h + 1 < XH:
                    x_queries(h + 1)
                for j in range(2):
                    dve.wait_ge(xt_hi_ok, 2 * h + j + 1)
                    dve.tensor_tensor(xpT_lo[:, j, :], ps[4 + j][:, :], fl(xpT_hi[:, j, :]), ALU.subtract).then_inc(xt_lo_ok, 1)
                if h + 2 < XH:
                    x_keys(h + 2)
                elif h + 2 == XH:
                    split_lo(U_XO + 1, 1)
                dve.wait_ge(xo_hi_ok, h + 1)
                dve.tensor_tensor(xo_lo[:, h, :], ps[6][:, :], fl(xo_hi[:, h, :]), ALU.subtract).then_inc(xo_lo_ok, 1)

            for v in range(4):
                if v >= 1:
                    split_lo(U_XO + v + 1, (v + 1) % 2)
                for b in range(2):
                    dve.wait_ge((xo_mm, unit_done)[b], (v + 1, U_XO + v + 1)[b])
                    residual(2 * v + b, 2 * (v % 2) + b)
                for b in range(2):
                    gained_lo(2 * v + b, R_FFN, 2 * KD + 2 * v + b + 1)

            split_lo(U_FFN + 1, 1)
            dve.wait_ge(rs_ok, N_X3 + 1)

            def ffn(i, head=False):
                for b in range(2):
                    m = 2 * i + b
                    if not (head and b == 0):
                        split_lo(U_FFN + 2 * m + 1, 1)
                    dve.wait_ge(unit_done, U_FFN + 2 * m + 1)
                    if not head:
                        dve.wait_ge(f_ok, m - 1)
                    dve.tensor_tensor(g_t[b][:, :], ps[2 * b][:, :], rs[:, :], ALU.mult).then_inc(evac, 1)
                    split_lo(U_FFN + 2 * m + 2, 0)
                    dve.wait_ge(unit_done, U_FFN + 2 * m + 2)
                    if not head:
                        dve.wait_ge(f_lo_ok, m - 1)
                    dve.tensor_tensor(u_t[b][:, :], ps[2 * b + 1][:, :], rs[:, :], ALU.mult).then_inc(evac, 1)
                    dve.wait_ge(silu_ok, m + 1)
                    dve.wait_ge(evac, G_FFN + 2 * m + 2)
                    dve.tensor_tensor(u_t[b][:, :], u_t[b][:, :], g_t[b][:, :], ALU.mult).then_inc(f_ok, 1)
                    dve.wait_ge(f_hi_ok, m + 1)
                    dve.tensor_tensor(tile(f_lo, m), u_t[b][:, :].rearrange("p (a n) -> p a n", a=1), fl(tile(f_hi, m)), ALU.subtract).then_inc(f_lo_ok, 1)
            ffn(0, head=True)
            repeat(dve, 1, KF // 2 - 1, ffn)

            for i in range(2):
                for k in range(4):
                    for j in range(3):
                        c = 3 * k + j + 1
                        if c < 12 or i == 0:
                            split_lo(U_DOWN + 12 * i + c, c % 2, P * DOWN_K[c % 3])
                    dve.wait_ge(unit_done, U_DOWN + 12 * i + 3 * k + 3)
                    residual(4 * i + k, k % 2)
            dve.wait_ge(rs_ok, N_X4 + 1)
            dve.reciprocal(stat[:, 4:8], stat[:, 0:4]).then_inc(y_rs, 1)
            dve.wait_ge(y_rs, 1)
            for t in range(NT):
                dve.tensor_scalar(y_nat[:, t, 0:S], y_nat[:, t, 0:S], stat[:, 4 + t:5 + t], None, ALU.mult).then_inc(y_left, 1)


_INS = ["x", "mem", "positions", "g_mix", "w_in", "b_gate", "g_q_lat", "w_uq", "g_kv_lat", "w_ukv", "w_a_proj",
        "w_b_proj", "w_o", "g_x", "g_mem", "w_xq", "w_xkv", "w_xo", "g_ffn", "w_gate", "w_up", "w_down", "g_final"]


def kernel(**inputs):
    import numpy as _np
    import concourse.bacc as _bacc
    from concourse import mybir as _mybir
    from concourse.bass_utils import run_bass_kernel_spmd as _run

    nc = _bacc.Bacc("TRN2", target_bir_lowering=False, num_devices=1)
    freq = (10000.0 ** (-_np.arange(0, ROPE, 2) / ROPE)).astype(_np.float32)
    arrays = {name: _np.ascontiguousarray(inputs[name]) for name in _INS}
    arrays["signed_freq"] = _np.concatenate([-freq, freq]).reshape(ROPE, 1)
    args = [nc.dram_tensor(f"in_{n}", a.shape, _mybir.dt.from_np(a.dtype), kind="ExternalInput").ap() for n, a in arrays.items()]
    args.append(nc.dram_tensor("out_y", (1, S, D), _mybir.dt.float32, kind="ExternalOutput").ap())
    build(nc, *args)
    r = _run(nc, [{f"in_{n}": a for n, a in arrays.items()}], core_ids=[0])
    return r.results[0]["out_y"]
```

```python
from contextlib import ExitStack

import concourse.bass as bass
import numpy as np
from concourse import mybir
from concourse.alu_op_type import AluOpType as ALU

F32 = mybir.dt.float32
F32R = mybir.dt.float32r
I32 = mybir.dt.int32
ACT = mybir.ActivationFunctionType
AX_X = mybir.AxisListType.X

P = 128
S = 512
D = 1024
KD = D // P
MEM = 256
NH = 8
NOPE, ROPE, DV = 64, 32, 64
QK = NOPE + ROPE
QR, KVR = 256, 128
SBH, SBD = 8, 64
XH, XD = 4, 128
FF = 2816
KF = FF // P
EPS = 1e-6
MLA_SCALE = QK ** -0.5
SB_SCALE = SBD ** -0.5
X_SCALE = XD ** -0.5
NEG = -1.0e30
HALF_PI = float(np.pi / 2)
KB = 1024
NT = S // P

C_CQ, C_CKV, C_KR = 0, QR, QR + KVR
C_SBQ = C_KR + ROPE
C_SBK = C_SBQ + SBH * SBD
C_SBV = C_SBK + SBH * SBD
C_GA = C_SBV + SBH * SBD

U_CQ, U_SB, U_GATE, U_MERGE, U_WO, U_XV, U_XKQ, U_XO, U_FFN, U_DOWN, U_END = (
    0, 4, 16, 32, 40, 48, 52, 60, 64, 108, 132)
G_CQ, G_SB, G_GATE, G_MERGE, G_WO, G_XKQ, G_XO, G_FFN, G_DOWN, G_END = (
    0, 4, 16, 32, 48, 56, 64, 72, 116, 124)
SB_FIRST = 3
SB_FILL = (2, 1, 1, 1, 1, 1, 1, 1)
Q_X, Q_CQ, Q_X2, Q_X3, Q_X4 = 0, 8, 10, 18, 26
N_X, N_CQ, N_CKV, N_X2, N_X3, N_X4 = 0, 1, 2, 3, 4, 5
Q0 = (0, 128, 256, 256)
OFF = (0, 512, 896, 1152)
CAUSAL = 1408
PT_STEP = 384
DOWN_K = (8, 8, 6)
R_MIX, R_X, R_MEM, R_FFN, R_FINAL, R_BIAS, R_Q, R_KV, R_ALL = 0, 8, 16, 24, 32, 40, 56, 58, 59


def build(nc, x, mem, positions, g_mix, w_in, b_gate, g_q_lat, w_uq, g_kv_lat, w_ukv, w_a_proj,
          w_b_proj, w_o, g_x, g_mem, w_xq, w_xkv, w_xo, g_ffn, w_gate, w_up, w_down, g_final,
          signed_freq, out):
    with ExitStack() as ctx:
        arena0 = 16512

        def sb(name, shape, dt, at):
            size = int(np.prod(shape[1:])) * 4
            assert arena0 + at + size <= 229344, (name, at, size)
            return nc.alloc_sbuf_tensor_at(name, shape, dt, offset=arena0 + at)

        def sem(name):
            return ctx.enter_context(nc.semaphore(name))

        h_hi = sb("h_hi", [P, KD, S], F32R, 0)
        h_lo = sb("h_lo", [P, KD, S], F32R, 16 * KB)
        xT = sb("xT", [P, KD, S], F32, 32 * KB)
        raw = [sb(f"raw{s}", [P, 1024], F32, (48 + 4 * s) * KB) for s in range(2)]
        w_hi = [sb(f"w_hi{s}", [P, 1024], F32R, (56 + 8 * s) * KB) for s in range(2)]
        w_lo = [sb(f"w_lo{s}", [P, 1024], F32R, (60 + 8 * s) * KB) for s in range(2)]
        fixed = [72 * KB]

        def small(name, cols, dt=F32):
            at = fixed[0]
            fixed[0] += (cols * 4 + 31) // 32 * 32
            assert fixed[0] <= 84 * KB
            return sb(name, [P, cols], dt, at)

        rs = small("rs", S)
        sq_sum = small("sq_sum", S)
        sq_tile = small("sq_tile", S)
        mask_row = small("mask_row", S)
        ident = small("ident", P)
        mask_kq = small("mask_kq", P)
        neg_tri = small("neg_tri", P, F32R)
        neg_ones = small("neg_ones", P, F32R)
        ones = small("ones", P)
        gains = small("gains", 64)
        consts = small("consts", 8)
        stat = small("stat", 16)
        stat_x = small("stat_x", 32)
        eps_c, half_pi_c, one_c = consts[:, 0:1], consts[:, 1:2], consts[:, 2:3]
        A0 = 84 * KB

        def area(name, shape, dt, kb):
            return sb(name, shape, dt, A0 + int(kb * KB))

        x_nat = area("x_nat", [P, NT, D], F32, 91)
        gain_rows = area("gain_rows", [P, P], F32, 81)
        scratch = area("scratch", [P, P], F32, 82)
        raw_more = [area(f"raw_more{n}", [P, 1024], F32, 4 * n) for n in range(2)]
        first_hi = [area(f"first_hi{n}", [P, 1024], F32R, 32 + 8 * n) for n in range(4)]
        first_lo = [area(f"first_lo{n}", [P, 1024], F32R, 36 + 8 * n) for n in range(4)]
        c_raw = area("c_raw", [P, 4, S], F32, 91)
        wu_raw = area("wu_raw", [P, 2560], F32, 107)
        cq_hi = area("cq_hi", [P, 2, S], F32R, 0)
        cq_lo = area("cq_lo", [P, 2, S], F32R, 4)
        ckv_hi = area("ckv_hi", [P, S], F32R, 8)
        ckv_lo = area("ckv_lo", [P, S], F32R, 10)
        wu_hi = area("wu_hi", [P, 2560], F32R, 12)
        wu_lo = area("wu_lo", [P, 2560], F32R, 22)
        q_hi = [area(f"q_hi{b}", [P, S], F32R, 32 + 4 * b) for b in range(2)]
        q_lo = [area(f"q_lo{b}", [P, S], F32R, 34 + 4 * b) for b in range(2)]
        k_hi = [area(f"k_hi{b}", [P, S], F32R, 40 + 4 * b) for b in range(2)]
        k_lo = [area(f"k_lo{b}", [P, S], F32R, 42 + 4 * b) for b in range(2)]
        va_hi = area("va_hi", [P, NT, S], F32R, 48)
        va_lo = area("va_lo", [P, NT, S], F32R, 56)
        probs = area("probs", [P, 1280], F32, 64)
        pT = area("pT", [P, 3584], F32R, 69)
        cos_t = area("cos_t", [P, S], F32, 83)
        sin_t = area("sin_t", [P, S], F32, 85)
        swapped = area("swapped", [P, S], F32, 87)
        roped = area("roped", [P, S], F32, 89)
        ang = area("ang", [P, S], F32, 64)
        turns = area("turns", [P, S], F32, 66)
        pos_i = area("pos_i", [P, S], I32, 69)
        rs_c = [area(f"rs_c{n}", [P, S], F32, 71 + 2 * n) for n in range(2)]
        c_norm = area("c_norm", [P, 3, S], F32, 75)
        sq_kv = area("sq_kv", [P, S], F32, 117)
        sbq = area("sbq", [P, 4, S], F32, 91)
        sbk = area("sbk", [P, 4, S], F32, 99)
        sbvT = area("sbvT", [P, 4, S], F32, 107)
        oa = area("oa", [P, 4, S], F32, 115)
        vb_hi = area("vb_hi", [P, NT, S], F32R, 0)
        vb_lo = area("vb_lo", [P, NT, S], F32R, 8)
        k_st = [area(f"k_st{b}", [P, S], F32R, 24 + 2 * b) for b in range(2)]
        qq_hi = [area(f"qq_hi{b}", [P, S], F32R, 16 + 4 * b) for b in range(2)]
        qq_lo = [area(f"qq_lo{b}", [P, S], F32R, 18 + 4 * b) for b in range(2)]
        stick = area("stick", [P, 1280], F32, 28)
        sp_hi = area("sp_hi", [P, CAUSAL], F32R, 33)
        sp_lo = area("sp_lo", [P, CAUSAL], F32R, 38.5)
        a_hi = area("a_hi", [P, CAUSAL], F32R, 44)
        a_lo = area("a_lo", [P, CAUSAL], F32R, 49.5)
        gates = area("gates", [P, 16, S], F32, 55)
        oa_hi = area("oa_hi", [P, 4, S], F32R, 99)
        oa_lo = area("oa_lo", [P, 4, S], F32R, 115)
        ob_hi = area("ob_hi", [P, 4, S], F32R, 107)
        ob_lo = area("ob_lo", [P, 4, S], F32R, 91)
        m_hi = area("m_hi", [P, KD, S], F32R, 32)
        m_lo = area("m_lo", [P, KD, S], F32R, 55)
        mem_nat = area("mem_nat", [P, 2, D], F32, 16)
        mem_junk = area("mem_junk", [P, D], F32, 24)
        mn_hi = area("mn_hi", [P, KD, MEM], F32R, 0)
        mn_lo = area("mn_lo", [P, KD, MEM], F32R, 8)
        xk_hi = area("xk_hi", [P, 4, MEM], F32R, 24)
        xk_lo = area("xk_lo", [P, 4, MEM], F32R, 28)
        xv_hi = area("xv_hi", [P, 2, S], F32R, 56)
        xv_lo = area("xv_lo", [P, 2, S], F32R, 60)
        xq_hi = area("xq_hi", [P, 4, S], F32R, 64)
        xq_lo = area("xq_lo", [P, 4, S], F32R, 72)
        xq_raw = [area(f"xq_raw{b}", [P, S], F32, 80 + 2 * b) for b in range(2)]
        xp = [area(f"xp{b}", [P, 4, MEM], F32, (84, 115)[b]) for b in range(2)]
        xpT_hi = area("xpT_hi", [P, 2, S], F32R, 16)
        xpT_lo = area("xpT_lo", [P, 2, S], F32R, 20)
        late_hi = [area(f"late_hi{n}", [P, 1024], F32R, 8 * n) for n in range(2)]
        late_lo = [area(f"late_lo{n}", [P, 1024], F32R, 4 + 8 * n) for n in range(2)]
        xo_hi = area("xo_hi", [P, 4, S], F32R, 91)
        xo_lo = area("xo_lo", [P, 4, S], F32R, 99)
        f_hi = area("f_hi", [P, KF, S], F32R, 0)
        f_lo = area("f_lo", [P, KF, S], F32R, 44)
        end_hi = sb("end_hi", [P, 1024], F32R, 0)
        end_lo = sb("end_lo", [P, 1024], F32R, 16 * KB)
        g_t = [area(f"g_t{b}", [P, S], F32, 107 + 2 * b) for b in range(2)]
        u_t = [area(f"u_t{b}", [P, S], F32, 111 + 2 * b) for b in range(2)]
        yT = area("yT", [P, 4, S], F32, 88)
        y_nat = area("y_nat", [P, NT, D], F32, 104)

        ps = [ctx.enter_context(nc.psum_tensor(f"ps{b}", [P, S], F32)) for b in range(8)]

        raw_in = [sem(f"raw_in{s}") for s in range(2)]
        more_in = [sem(f"more_in{n}") for n in range(2)]
        hi_done = sem("hi_done")
        lo_done = sem("lo_done")
        unit_done = sem("unit_done")
        evac = sem("evac")
        x_in = [sem(f"x_in{q}") for q in range(4)]
        gain_mix_in, gains_in = sem("gain_mix_in"), sem("gains_in")
        pos_in, freq_in = sem("pos_in"), sem("freq_in")
        wu_in, mem_in = sem("wu_in"), sem("mem_in")
        y_out = sem("y_out")
        pool_const = sem("pool_const")
        const_r = sem("const_r")
        gains_T, gains_ok = sem("gains_T"), sem("gains_ok")
        dve_step, act_step, pool_step = sem("dve_step"), sem("act_step"), sem("pool_step")
        x_T, x_kept = sem("x_T"), sem("x_kept")
        h_hi_ok, h_lo_ok = sem("h_hi_ok"), sem("h_lo_ok")
        sq_ok, sq_added = sem("sq_ok"), sem("sq_added")
        sum_clear = sem("sum_clear")
        sq_kv_ok = sem("sq_kv_ok")
        stat_ok = sem("stat_ok")
        ln_ok, rs_ok = sem("ln_ok"), sem("rs_ok")
        trig_arg, trig_ok = sem("trig_arg"), sem("trig_ok")
        wu_hi_ok, wu_lo_ok = sem("wu_hi_ok"), sem("wu_lo_ok")
        cn_ok, c_hi_ok, c_lo_ok = sem("cn_ok"), sem("c_hi_ok"), sem("c_lo_ok")
        kr_ok, kr_hi_ok, kr_lo_ok = sem("kr_ok"), sem("kr_hi_ok"), sem("kr_lo_ok")
        va_mm, va_hi_ok, va_lo_ok = sem("va_mm"), sem("va_hi_ok"), sem("va_lo_ok")
        proj_mm = sem("proj_mm")
        dve_rope, rope_ok = sem("dve_rope"), sem("rope_ok")
        qk_hi_ok, qk_lo_ok = sem("qk_hi_ok"), sem("qk_lo_ok")
        rope_lo_ok = sem("rope_lo_ok")
        s_mm, s_ok = sem("s_mm"), sem("s_ok")
        e_ok, r_ok, p_ok = sem("e_ok"), sem("r_ok"), sem("p_ok")
        t_mm, pt_hi_ok, pt_lo_ok = sem("t_mm"), sem("pt_hi_ok"), sem("pt_lo_ok")
        pt_zero_ok = sem("pt_zero_ok")
        pv_mm, o_ok = sem("pv_mm"), sem("o_ok")
        sp_zero_ok = sem("sp_zero_ok")
        vT_mm, vb_hi_ok, vb_lo_ok = sem("vT_mm"), sem("vb_hi_ok"), sem("vb_lo_ok")
        qk_b_hi_ok, qk_b_lo_ok = sem("qk_b_hi_ok"), sem("qk_b_lo_ok")
        z_mm, z_ok, l_ok = sem("z_mm"), sem("z_ok"), sem("l_ok")
        sp_ok, sp_hi_ok, sp_lo_ok = sem("sp_ok"), sem("sp_hi_ok"), sem("sp_lo_ok")
        w_mm, a_ok = sem("w_mm"), sem("a_ok")
        a_hi_ok, a_lo_ok = sem("a_hi_ok"), sem("a_lo_ok")
        pvb_mm, ob_hi_ok, ob_ok = sem("pvb_mm"), sem("ob_hi_ok"), sem("ob_ok")
        sig_ok, oa_hi_ok, oa_lo_ok = sem("sig_ok"), sem("oa_hi_ok"), sem("oa_lo_ok")
        m_ok, m_hi_ok, m_lo_ok = sem("m_ok"), sem("m_hi_ok"), sem("m_lo_ok")
        mem_sq, mem_rs, mem_n = sem("mem_sq"), sem("mem_rs"), sem("mem_n")
        mem_T, mn_hi_ok, mn_lo_ok = sem("mem_T"), sem("mn_hi_ok"), sem("mn_lo_ok")
        xv_hi_ok, xv_lo_ok = sem("xv_hi_ok"), sem("xv_lo_ok")
        xk_hi_ok = sem("xk_hi_ok")
        xq_hi_ok, xq_lo_ok = sem("xq_hi_ok"), sem("xq_lo_ok")
        xs_mm, xs_max, xe_ok, xp_ok = map(sem, ("xs_mm", "xs_max", "xe_ok", "xp_ok"))
        xt_mm, xt_hi_ok, xt_lo_ok = sem("xt_mm"), sem("xt_hi_ok"), sem("xt_lo_ok")
        xpv_mm, xo_hi_ok, xo_lo_ok = sem("xpv_mm"), sem("xo_hi_ok"), sem("xo_lo_ok")
        xo_mm = sem("xo_mm")
        silu_ok, f_ok = sem("silu_ok"), sem("f_ok")
        f_hi_ok, f_lo_ok = sem("f_hi_ok"), sem("f_lo_ok")
        end_mm, end_ok = sem("end_mm"), sem("end_ok")
        y_ok = sem("y_ok")
        yT_mm, y_rs = sem("yT_mm"), sem("y_rs")
        y_left, y_right = sem("y_left"), sem("y_right")

        def fl(ap):
            return ap.bitcast(F32)

        def tile(t, m, n=1):
            return t[:, m:m + n, :] if isinstance(m, int) else t[:, bass.ds(m, n), :]

        def col(t, m):
            return t[:, m:m + 1] if isinstance(m, int) else t[:, bass.ds(m, 1)]

        def bank(b, n=1, w=S):
            return ps[b][:, 0:w].rearrange("p (a n) -> p a n", a=n)

        def cols(base, m, w=P):
            return base[:, :, m:m + w] if isinstance(m, int) else base[:, :, bass.ds(m, w)]

        def repeat(eng, first, n, body):
            with eng.Fori(first, first + n) as i:
                body(i)

        class Steps:

            def __init__(self, eng, s):
                self.eng, self.sem, self.n = eng, s, 0

            def link(self, ins):
                ins.then_inc(self.sem, 1)
                self.n += 1
                self.eng.wait_ge(self.sem, self.n)

        w_in_v = w_in[0].rearrange("(k p) n -> p k n", p=P)

        fills, u = [], U_SB + SB_FIRST
        for n in SB_FILL:
            fills.append(list(range(u, u + n)))
            u += n

        S_BANK, S_COL = (2, 2, 3, 7), (0, 256, 0, 0)
        P_AT = (0, 128, 384, 768)
        T_BANK, T_COL = (4, 4, 5, 6), (0, 128, 0, 0)
        VA_BANK, V_BANK = (2, 3, 6, 7), (1, 7)
        FIRST_HI = (1, 3, 4)
        BEHIND = (0, 2, 4, 5)
        XO_BANK = (0, 1, 7, 3, 2, 4, 5, 6)
        END_BANKS = (1, 6)
        S_AT = (0, 512, 896, 1152)
        DONE = (1, 1, 2, 3)

        block = ctx.enter_context(nc.Block())

        @block.sync
        def _(sp):
            def load3(u, s, src, k, free=None):
                sp.wait_ge(lo_done, u - 1 if free is None else free)
                w = src.shape[2]
                sp.dma_start(raw[s][:, 0:k * w].rearrange("p (k n) -> p k n", k=k), src).then_inc(raw_in[s], 16)

            for n, (c, w) in enumerate(((C_CQ, P), (C_CQ + P, P), (C_CKV, P), (C_KR - NOPE, QK))):
                if n == 2:
                    sp.wait_ge(x_in[-1], 16)
                dst = (raw + raw_more)[n][:, 0:KD * w].rearrange("p (k n) -> p k n", k=KD)
                sp.dma_start(dst, cols(w_in_v, c, w)).then_inc((raw_in + more_in)[n], 16)
                if n == 0:
                    sp.dma_start(gain_rows[0:8, :], g_mix[0].rearrange("(k p) -> k p", p=P)).then_inc(gain_mix_in, 16)
            rows = ((g_x[0], R_X, 8), (g_mem[0], R_MEM, 8), (g_ffn[0], R_FFN, 8), (g_final, R_FINAL, 8),
                    (b_gate[0].rearrange("a n -> (a n)"), R_BIAS, 16), (g_q_lat[0], R_Q, 2), (g_kv_lat[0], R_KV, 1))
            for src, row, count in rows:
                sp.dma_start(gain_rows[row:row + count, :], src.rearrange("(k p) -> k p", p=P)).then_inc(gains_in, 16)
            sp.dma_start(wu_raw[:, 0:1536].rearrange("p (k n) -> p k n", k=2),
                         w_uq[0].rearrange("(k p) n -> p k n", p=P)).then_inc(wu_in, 16)
            sp.dma_start(wu_raw[:, 1536:2560], w_ukv[0]).then_inc(wu_in, 16)
            for s in range(2):
                load3(U_SB + s, s, cols(w_in_v, C_SBQ + P * s), KD, free=s + 1)

            def in_pair(i):
                for s in range(2):
                    load3(U_SB + 2 * i + s, s, cols(w_in_v, C_SBQ + 2 * P * i + P * s), KD)
            repeat(sp, 1, (U_MERGE - U_SB) // 2 - 1, in_pair)

            a_v = w_a_proj[0].rearrange("(k p) n -> p k n", p=P)
            b_v = w_b_proj[0].rearrange("(k p) n -> p k n", p=P)

            def merge(t):
                load3(U_MERGE + 2 * t, 0, cols(a_v, 2 * P * t, 2 * P), 4)
                load3(U_MERGE + 2 * t + 1, 1, cols(b_v, 2 * P * t, 2 * P), 4)
            repeat(sp, 0, 4, merge)

            def square(base, w):
                v = w[0].rearrange("(k p) n -> p k n", p=P)

                def body(i):
                    for s in range(2):
                        load3(base + 2 * i + s, s, cols(v, 2 * P * i + P * s), KD)
                return body
            repeat(sp, 0, 4, square(U_WO, w_o))
            xkv_v = w_xkv[0].rearrange("(k p) n -> p k n", p=P)
            xq_v = w_xq[0].rearrange("(k p) n -> p k n", p=P)
            for j in range(4):
                load3(U_XV + j, j % 2, xkv_v[:, 2 * j:2 * j + 2, XH * XD:2 * XH * XD], 2)

            def x_head(h):
                load3(U_XKQ + 2 * h, 0, cols(xkv_v, XD * h), KD)
                load3(U_XKQ + 2 * h + 1, 1, cols(xq_v, XD * h), KD)
            repeat(sp, 0, XH, x_head)
            xo_v = w_xo[0].rearrange("(k p) n -> p k n", p=P)

            def xo_pair(i):
                for s in range(2):
                    load3(U_XO + 2 * i + s, s, cols(xo_v, 4 * P * i + 2 * P * s, 2 * P), 4)
            repeat(sp, 0, 2, xo_pair)
            gate_v = w_gate[0].rearrange("(k p) n -> p k n", p=P)
            up_v = w_up[0].rearrange("(k p) n -> p k n", p=P)

            def ffn(m):
                load3(U_FFN + 2 * m, 0, cols(gate_v, P * m), KD)
                load3(U_FFN + 2 * m + 1, 1, cols(up_v, P * m), KD)
            repeat(sp, 0, KF, ffn)
            down_v = w_down[0].rearrange("(k p) n -> p k n", p=P)

            def down(i):
                for j in range(6):
                    k0 = sum(DOWN_K[:j % 3])
                    k = DOWN_K[j % 3]
                    load3(U_DOWN + 6 * i + j, j % 2, cols(down_v[:, k0:k0 + k, :], 2 * P * i + P * (j // 3)), k)
            repeat(sp, 0, 4, down)

            for t in range(NT):
                sp.wait_ge(y_left, t + 1)
                sp.wait_ge(y_right, t + 1)
                sp.dma_start(out[0, t * P:(t + 1) * P, :], y_nat[:, t, :]).then_inc(y_out, 16)
            sp.wait_ge(y_out, 16 * NT)

        @block.tensor
        def _(pe):
            def three(acc, l_hi, l_lo, r_hi, r_lo, start, stop):
                pe.matmul(acc, l_hi, r_hi, start=start, stop=False)
                pe.matmul(acc, l_hi, r_lo, start=False, stop=False)
                return pe.matmul(acc, l_lo, r_hi, start=False, stop=stop)

            def gemm(u, s, banks, kts, r_hi, r_lo, width=P, n=S, start=True, stop=True, k0=0, ready=None, free=None):
                pe.wait_ge(lo_done, u + 1)
                m = len(banks)
                for b, dst in enumerate(banks):
                    if free:
                        free(b)
                    for k in range(kts):
                        if ready and b == 0:
                            ready(k)
                        c = (k * m + b) * width
                        last = three(ps[dst][0:width, 0:n], w_hi[s][:, c:c + width], w_lo[s][:, c:c + width],
                                     r_hi[:, k0 + k, :], r_lo[:, k0 + k, :],
                                     start and k == 0, stop and k == kts - 1)
                last.then_inc(unit_done, 1)

            def statistic(n, squares):
                pe.wait_ge(sq_added, squares)
                pe.matmul(ps[7][:, :], ones[:, :], sq_sum[:, :], start=True, stop=True).then_inc(stat_ok, 1)

            pe.wait_ge(pool_const, 4)
            pe.wait_ge(gain_mix_in, 16)
            pe.transpose(ps[7][:, 0:8], gain_rows[0:8, :], ident[0:8, 0:8]).then_inc(gains_T, 1)
            def x_transposes(m):
                pe.wait_ge(x_in[m // 2], 16)
                if m >= 3:
                    pe.wait_ge(h_lo_ok, m - 2)
                for t in range(NT):
                    last = pe.transpose(ps[4 + m % 3][:, t * P:(t + 1) * P], x_nat[:, t, m * P:(m + 1) * P], ident[:, :])
                last.then_inc(x_T, 1)
            x_transposes(0)
            x_transposes(1)

            def first_unit(n, k):
                if k == 0:
                    pe.wait_ge(lo_done, n + 1)
                w = QK if n == 3 else P
                last = three(ps[n][0:w, :], first_hi[n][:, k * w:(k + 1) * w], first_lo[n][:, k * w:(k + 1) * w],
                             h_hi[:, k, :], h_lo[:, k, :], k == 0, k == KD - 1)
                if k == KD - 1:
                    last.then_inc(unit_done, 1)

            for step in range(KD + BEHIND[-1]):
                if step + 2 < KD:
                    x_transposes(step + 2)
                if step < KD:
                    pe.wait_ge(h_lo_ok, step + 1)
                for n, behind in enumerate(BEHIND):
                    if 0 <= step - behind < KD:
                        first_unit(n, step - behind)
                if step == KD:
                    pe.wait_ge(gains_ok, 1)
                    statistic(N_X, Q_CQ)
                    pe.wait_ge(gains_in, 16 * 7)
                    pe.transpose(ps[6][:, 0:R_ALL], gain_rows[0:R_ALL, :], ident[0:R_ALL, 0:R_ALL]).then_inc(gains_T, 1)

            def filler(u, b=None, read_out=None):
                pe.wait_ge(evac, u - 1 if read_out is None else read_out)
                gemm(u, u % 2, [u % 2 if b is None else b], KD, h_hi, h_lo)

            pe.wait_ge(x_kept, KD)
            gemm(4, 0, [4], KD, h_hi, h_lo)
            pe.wait_ge(rs_ok, 1)
            statistic(N_CQ, Q_X2)
            pe.wait_ge(sq_kv_ok, 1)
            pe.wait_ge(gains_ok, 2)
            pe.matmul(ps[6][:, :], ones[:, :], sq_kv[:, :], start=True, stop=True).then_inc(stat_ok, 1)
            gemm(5, 1, [5], KD, h_hi, h_lo)
            filler(6, read_out=1)
            pe.wait_ge(wu_lo_ok, 1)
            pe.wait_ge(c_lo_ok, 3)
            v_hi_w = wu_hi[:, 1536:2560].rearrange("p (h d) -> p h d", h=NH)[:, :, NOPE:NOPE + DV]
            v_lo_w = wu_lo[:, 1536:2560].rearrange("p (h d) -> p h d", h=NH)[:, :, NOPE:NOPE + DV]
            pe.wait_ge(evac, 4)
            pe.wait_ge(rs_ok, 3)
            for t in range(NT):
                c = slice(t * P, (t + 1) * P)
                three(bank(VA_BANK[t], NH), ckv_hi[:, c], ckv_lo[:, c], v_hi_w, v_lo_w, True, True).then_inc(va_mm, 1)

            def mla_proj(h):
                for k in range(2):
                    c = k * 768 + h * QK
                    last = three(ps[4][0:QK, :], wu_hi[:, c:c + QK], wu_lo[:, c:c + QK],
                                 cq_hi[:, k, :], cq_lo[:, k, :], k == 0, k == 1)
                last.then_inc(proj_mm, 1)
                c = 1536 + h * (NOPE + DV)
                three(ps[5][0:NOPE, :], wu_hi[:, c:c + NOPE], wu_lo[:, c:c + NOPE],
                      ckv_hi[:, :], ckv_lo[:, :], True, True).then_inc(proj_mm, 1)

            def mla_scores(h):
                pe.wait_ge(qk_lo_ok, 2 * h + 2)
                pe.wait_ge(rope_lo_ok, h + 1)
                b = h % 2
                for i in range(NT):
                    n = max(256, (i + 1) * P)
                    if h >= 1:
                        pe.wait_ge(s_ok, 4 * h)
                    elif i == 0:
                        pe.wait_ge(va_lo_ok, NT)
                    elif i == 3:
                        pe.wait_ge(rs_ok, 2)
                    c = slice(i * P, (i + 1) * P)
                    last = three(ps[S_BANK[i]][:, S_COL[i]:S_COL[i] + n], q_hi[b][0:QK, c], q_lo[b][0:QK, c],
                                 k_hi[b][0:QK, 0:n], k_lo[b][0:QK, 0:n], True, True)
                    if i >= 1:
                        last.then_inc(s_mm, 1)

            def mla_transposes(h):
                pe.wait_ge(qk_lo_ok, min(2 * h + 4, 2 * NH))
                if h >= 1:
                    pe.wait_ge(o_ok, h)
                else:
                    pe.wait_ge(rs_ok, 3)
                for i in range(NT):
                    pe.wait_ge(p_ok, 4 * h + i + 1)
                    for j in range(i + 1):
                        c, at = T_COL[i] + j * P, P_AT[i] + j * P
                        last = pe.transpose(ps[T_BANK[i]][:, c:c + P], probs[:, at:at + P], ident[:, :])
                    if i >= 1:
                        last.then_inc(t_mm, 1)

            def pv(dst, v_hi_t, v_lo_t, h, r_hi, r_lo):
                c = slice(h // 2 * P, h // 2 * P + P)
                for j in range(NT):
                    last = three(ps[dst][:, Q0[j]:S], v_hi_t[:, j, c], v_lo_t[:, j, c], r_hi(j), r_lo(j), j == 0, j == NT - 1)
                return last

            def mla_pv(h):
                pe.wait_ge(pt_lo_ok, 4 * h + 4)
                if h == 0:
                    pe.wait_ge(pt_zero_ok, 2)
                pv(6, va_hi, va_lo, h, lambda j: pT[:, j * PT_STEP + Q0[j]:j * PT_STEP + S],
                   lambda j: pT[:, 1664 + j * PT_STEP + Q0[j]:1664 + j * PT_STEP + S]).then_inc(pv_mm, 1)

            def sb_scores(h, tiles=(3, 2, 1, 0)):
                pe.wait_ge(qk_b_lo_ok, 4 * h + 4)
                b = h % 2
                for j in tiles:
                    n = NT - 1 - j
                    if h >= 1:
                        pe.wait_ge(a_ok, 4 * (h - 1) + n + 1)
                    elif n == 2:
                        pe.wait_ge(pt_lo_ok, 4 * NH)
                    acc, k_tile = ps[5 - j][:, 0:S - Q0[j]], k_st[b][:, j * P:(j + 1) * P]
                    pe.matmul(acc, k_tile, qq_hi[b][:, Q0[j]:S], start=True, stop=False)
                    pe.matmul(acc, k_tile, qq_lo[b][:, Q0[j]:S], start=False, stop=True).then_inc(z_mm, 1)

            pe.wait_ge(c_lo_ok, 3)
            pe.wait_ge(evac, 6)
            mla_proj(0)
            filler(7, read_out=2)
            for h in range(NH):
                mla_scores(h)
                if h + 1 < NH:
                    if h == 0:
                        pe.wait_ge(qk_lo_ok, 2)
                    else:
                        pe.wait_ge(pt_lo_ok, 4 * h)
                    mla_proj(h + 1)
                if h >= 1:
                    mla_pv(h - 1)
                filler(fills[h][-1])
                if h + 1 == NH:
                    pe.wait_ge(s_ok, 4 * NH)
                    sb_scores(0, (3, 2))
                mla_transposes(h)

            def v_transposes(tiles):
                for t in tiles:
                    if t >= 2:
                        pe.wait_ge(vb_lo_ok, t - 1)
                    else:
                        pe.wait_ge(evac, G_GATE)
                    for j in range(4):
                        last = pe.transpose(ps[V_BANK[t % 2]][:, j * P:(j + 1) * P], sbvT[:, j, t * P:(t + 1) * P], ident[:, :])
                    last.then_inc(vT_mm, 1)

            def sb_suffix(h):
                for n, j in enumerate((3, 2, 1, 0)):
                    pe.wait_ge(sp_lo_ok, 4 * h + n + 1)
                    w = S - Q0[j]
                    for part in (sp_hi, sp_lo):
                        last = pe.matmul(ps[5 - j][:, 0:w], neg_tri[:, :], part[:, OFF[j]:OFF[j] + w],
                                         start=False, stop=True, skip_group_check=True)
                        for k in range(j + 1, NT):
                            last = pe.matmul(ps[5 - j][:, Q0[k] - Q0[j]:w], neg_ones[:, :],
                                             part[:, OFF[k]:OFF[k] + S - Q0[k]],
                                             start=False, stop=True, skip_group_check=True)
                    last.then_inc(w_mm, 1)

            def sb_pv(h):
                pe.wait_ge(a_lo_ok, 4 * h + 4)
                if h >= 1:
                    pe.wait_ge(ob_ok, h)
                else:
                    pe.wait_ge(vb_lo_ok, NT)
                pv(6, vb_hi, vb_lo, h, lambda j: a_hi[:, OFF[j]:OFF[j] + S - Q0[j]],
                   lambda j: a_lo[:, OFF[j]:OFF[j] + S - Q0[j]]).then_inc(pvb_mm, 1)

            v_transposes((0, 1))
            sb_scores(0, (1, 0))
            gemm(U_GATE, 0, [0], KD, h_hi, h_lo)
            mla_pv(NH - 1)
            v_transposes((2, 3))
            pe.wait_ge(sp_zero_ok, 1)
            for h in range(SBH):
                u = U_GATE + 2 * h
                if h >= 1:
                    sb_scores(h)
                    sb_pv(h - 1)
                    filler(u)
                sb_suffix(h)
                if h == 0:
                    pe.wait_ge(vb_lo_ok, 3)
                    pe.wait_ge(sp_zero_ok, 2)
                filler(u + 1)

            pe.wait_ge(oa_lo_ok, 2)
            gemm(U_MERGE, 0, [0, 1], 4, oa_hi, oa_lo, free=lambda b: pe.wait_ge(evac, G_MERGE - 1 + b))
            sb_pv(SBH - 1)
            gemm(U_MERGE + 1, 1, [2, 3], 4, ob_hi, ob_lo, ready=lambda k: pe.wait_ge(ob_ok, 2 * k + 2))

            def merge(t):
                pe.wait_ge(evac, G_MERGE + 4 * t - 2)
                gemm(U_MERGE + 2 * t, 0, [0, 1], 4, oa_hi, oa_lo)
                pe.wait_ge(evac, G_MERGE + 4 * t)
                gemm(U_MERGE + 2 * t + 1, 1, [2, 3], 4, ob_hi, ob_lo)
            repeat(pe, 1, 3, merge)

            def wo(i):
                for s in range(2):
                    pe.wait_ge(evac, G_WO - 1 + 2 * i + s)
                    gemm(U_WO + 2 * i + s, s, [s], KD, m_hi, m_lo)
            pe.wait_ge(evac, G_WO - 2)
            for tiles in (range(6), range(6, KD)):
                for s in range(2):
                    pe.wait_ge(lo_done, U_WO + s + 1)
                    for k in tiles:
                        if s == 0:
                            pe.wait_ge(m_lo_ok, k + 1)
                        c = slice(k * P, (k + 1) * P)
                        last = three(ps[s][:, :], w_hi[s][:, c], w_lo[s][:, c], m_hi[:, k, :], m_lo[:, k, :],
                                     k == 0, k == KD - 1)
                    if tiles[-1] == KD - 1:
                        last.then_inc(unit_done, 1)
            pe.wait_ge(mem_n, 2)
            for m in range(KD):
                for t in range(2):
                    c = m % 2 * MEM + t * P
                    last = pe.transpose(ps[4 + m // 2][:, c:c + P], mem_nat[:, t, m * P:(m + 1) * P], ident[:, :])
                if m % 2:
                    last.then_inc(mem_T, 1)
            repeat(pe, 1, 3, wo)

            pe.wait_ge(mn_lo_ok, KD)
            for j in range(4):
                u, s = U_XV + j, j % 2
                pe.wait_ge(lo_done, u + 1)
                for k in range(2):
                    w = slice(k * S, (k + 1) * S)
                    for t in range(2):
                        c = slice(t * P, (t + 1) * P)
                        last = three(ps[4 + t][:, :], mn_hi[:, 2 * j + k, c], mn_lo[:, 2 * j + k, c],
                                     w_hi[s][:, w], w_lo[s][:, w], j == 0 and k == 0, j == 3 and k == 1)
                last.then_inc(unit_done, 1)
                if j == 1:
                    statistic(N_X2, Q_X3)

            def x_keys(h):
                pe.wait_ge(evac, G_XKQ + 2 * h - 1)
                gemm(U_XKQ + 2 * h, 0, [0], KD, mn_hi, mn_lo, n=MEM)

            def x_queries(h):
                pe.wait_ge(evac, G_XKQ + 2 * h)
                gemm(U_XKQ + 2 * h + 1, 1, [1], KD, h_hi, h_lo)

            def x_scores(h):
                pe.wait_ge(xq_lo_ok, h + 1)
                pe.wait_ge(evac, G_XKQ + 2 * h + 1)
                for i in range(NT):
                    if h >= 1 and i % 2 == 0:
                        pe.wait_ge(xe_ok, 4 * (h - 1) + i + 2)
                    c = slice(i * P, (i + 1) * P)
                    last = three(ps[2 + i // 2][:, i % 2 * MEM:(i % 2 + 1) * MEM], xq_hi[:, h, c], xq_lo[:, h, c],
                                 xk_hi[:, h, :], xk_lo[:, h, :], True, True)
                    if i % 2:
                        last.then_inc(xs_mm, 1)

            def x_transposes_of(h):
                for j in range(2):
                    pe.wait_ge(xp_ok, 4 * h + 4)
                    if h >= 1:
                        pe.wait_ge(xt_lo_ok, 2 * h - 1 + j)
                    else:
                        pe.wait_ge(xv_lo_ok, 2)
                    for i in range(NT):
                        last = pe.transpose(ps[4 + j][:, i * P:(i + 1) * P], xp[h % 2][:, i, j * P:(j + 1) * P], ident[:, :])
                    last.then_inc(xt_mm, 1)

            def x_pv(h):
                pe.wait_ge(xt_lo_ok, 2 * h + 2)
                if h >= 1:
                    pe.wait_ge(xo_lo_ok, h)
                c = slice(h * XD, (h + 1) * XD)
                for j in range(2):
                    last = three(ps[6][:, :], xv_hi[:, j, c], xv_lo[:, j, c], xpT_hi[:, j, :], xpT_lo[:, j, :], j == 0, j == 1)
                last.then_inc(xpv_mm, 1)

            def xo_part(v, heads, tiles=(0, 1)):
                hi, lo = (w_hi + late_hi)[v], (w_lo + late_lo)[v]
                for b in tiles:
                    for k in heads:
                        pe.wait_ge(xo_lo_ok, k + 1)
                        c = (2 * k + b) * P
                        last = three(ps[XO_BANK[2 * v + b]][:, :], hi[:, c:c + P], lo[:, c:c + P],
                                     xo_hi[:, k, :], xo_lo[:, k, :], k == 0, k == XH - 1)
                    if heads[-1] == XH - 1:
                        last.then_inc((xo_mm, unit_done)[b], 1)

            x_keys(0)
            pe.wait_ge(h_lo_ok, 2 * KD)
            x_queries(0)
            x_keys(1)
            x_scores(0)
            x_queries(1)
            x_transposes_of(0)
            x_keys(2)
            x_pv(0)
            x_scores(1)
            x_queries(2)
            x_transposes_of(1)
            x_keys(3)
            x_pv(1)
            x_scores(2)
            x_queries(3)
            x_transposes_of(2)
            pe.wait_ge(lo_done, U_XO + 1)
            pe.wait_ge(evac, G_XO)
            xo_part(0, [0, 1])
            x_pv(2)
            x_scores(3)
            xo_part(0, [2])
            pe.wait_ge(lo_done, U_XO + 2)
            xo_part(1, [0, 1, 2], (0,))
            x_transposes_of(3)
            pe.wait_ge(xe_ok, 4 * XH)
            xo_part(1, [0, 1, 2], (1,))
            x_pv(3)
            pe.wait_ge(lo_done, U_XO + 3)
            xo_part(2, [0, 1, 2])
            for v in range(3):
                xo_part(v, [3])
            pe.wait_ge(lo_done, U_XO + 4)
            xo_part(3, [0, 1, 2, 3])

            def ffn(i):
                for b in range(2):
                    pe.wait_ge(evac, G_FFN - 2 + 4 * i + 2 * b)
                    gemm(U_FFN + 4 * i + 2 * b, 0, [2 * b], KD, h_hi, h_lo)
                    gemm(U_FFN + 4 * i + 2 * b + 1, 1, [2 * b + 1], KD, h_hi, h_lo)
            pe.wait_ge(evac, G_XO + 2)
            gemm(U_FFN, 0, [0], KD, h_hi, h_lo, ready=lambda k: pe.wait_ge(h_lo_ok, 2 * KD + k + 1))
            gemm(U_FFN + 1, 1, [1], KD, h_hi, h_lo)
            statistic(N_X3, Q_X4)
            pe.wait_ge(evac, G_FFN)
            gemm(U_FFN + 2, 0, [2], KD, h_hi, h_lo)
            gemm(U_FFN + 3, 1, [3], KD, h_hi, h_lo)
            repeat(pe, 1, KF // 2 - 1, ffn)

            def y_transposes(m, tiles=range(NT)):
                k = m % 4
                for t in tiles:
                    last = pe.transpose(ps[2 + t][:, k * P:(k + 1) * P], yT[:, k, t * P:(t + 1) * P], ident[:, :])
                if k == 3:
                    last.then_inc(yT_mm, 1)

            for m in range(KD - 1):
                pe.wait_ge(evac, G_DOWN - 1 + m)
                for j in range(3):
                    pe.wait_ge(f_lo_ok, KF if j == 2 else 2 * DOWN_K[0])
                    gemm(U_DOWN + 3 * m + j, (3 * m + j) % 2, [m % 2], DOWN_K[j], f_hi, f_lo,
                         start=j == 0, stop=j == 2, k0=sum(DOWN_K[:j]))
                    if j == 0 and m >= 1:
                        pe.wait_ge(y_ok, m + (4 if m > 4 else 0))
                        y_transposes(m - 1)

            def end_statistic(half):
                pe.wait_ge(sq_added, Q_X4 + KD - 1)
                pe.wait_ge(sq_ok, Q_X4 + KD + half)
                for t in (2 * half, 2 * half + 1):
                    c = slice(t * P, (t + 1) * P)
                    pe.matmul(ps[7][:, t:t + 1], sq_sum[:, c], ones[:, 0:1], start=True, stop=False)
                    last = pe.matmul(ps[7][:, t:t + 1], sq_tile[:, c], ones[:, 0:1], start=False, stop=True)
                last.then_inc(stat_ok, 1)
                pe.wait_ge(y_ok, KD + 4 + half)
                y_transposes(KD - 1, (2 * half, 2 * half + 1))

            pe.wait_ge(evac, G_END - 2)
            for half in range(2):
                tokens = slice(half * MEM, (half + 1) * MEM)
                for j in range(3):
                    slot = (3 * (KD - 1) + j) % 2
                    hi, lo = (end_hi, end_lo) if j == 2 else (w_hi[slot], w_lo[slot])
                    pe.wait_ge(lo_done, U_END - 2 + j)
                    for k in range(DOWN_K[j]):
                        c, kf = slice(k * P, (k + 1) * P), sum(DOWN_K[:j]) + k
                        last = three(ps[END_BANKS[half]][:, 0:MEM], hi[:, c], lo[:, c], f_hi[:, kf, tokens],
                                     f_lo[:, kf, tokens], kf == 0, kf == KF - 1)
                    if j == 0 and half == 0:
                        pe.wait_ge(y_ok, KD + 3)
                        y_transposes(KD - 2)
                    if j == 0 and half == 1:
                        end_statistic(0)
                last.then_inc(end_mm, 1)
            end_statistic(1)

        @block.scalar
        def _(act):
            steps = Steps(act, act_step)

            def exp_and_ln():
                act.preload_act_table_set("natural_log_exp_and_others")

            def split_first(n):
                act.wait_ge((raw_in + more_in)[n], 16)
                w = KD * (QK if n == 3 else P)
                act.activation(first_hi[n][:, 0:w], (raw + raw_more)[n][:, 0:w], ACT.Copy).then_inc(hi_done, 1)

            def split_hi(u, s, n=1024, fresh=False, used=None):
                act.wait_ge(raw_in[s], 8 * (u - s))
                if not fresh:
                    act.wait_ge(unit_done, used or u - 1)
                act.activation(w_hi[s][:, 0:n], raw[s][:, 0:n], ACT.Copy).then_inc(hi_done, 1)

            def square(n, src):
                if not isinstance(n, int) or n > 0:
                    act.wait_ge(sq_added, n)
                act.activation(sq_tile[:, :].rearrange("p (a n) -> p a n", a=1), src, ACT.Square).then_inc(sq_ok, 1)

            def inv_rms(n, dst, size, between=None):
                act.wait_ge(stat_ok, n + 1)
                act.activation(dst, ps[7][:, :], ACT.Ln, scale=1.0 / size, bias=eps_c).then_inc(ln_ok, 1)
                act.wait_ge(ln_ok, n + 1)
                if between:
                    between()
                exp_and_ln()
                act.activation(dst, dst, ACT.Exp, scale=-0.5).then_inc(rs_ok, 1)

            for q in range(4):
                c = slice(q * 2 * P, (q + 1) * 2 * P)
                act.dma_start(x_nat[:, :, c], x[0, :, c].rearrange("(t p) d -> p t d", p=P)).then_inc(x_in[q], 16)
            split_first(0)
            act.wait_ge(gains_ok, 1)

            def gained(dst, m, src, row, ok):
                act.activation(tile(dst, m), src, ACT.Copy, scale=col(gains, row + m)).then_inc(ok, 1)

            for m in range(KD):
                act.wait_ge(x_kept, m + 1)
                gained(h_hi, m, tile(xT, m), R_MIX, h_hi_ok)
                if m in FIRST_HI:
                    split_first(FIRST_HI.index(m) + 1)
                if m >= 1:
                    square(Q_X + m - 1, tile(xT, m - 1))
            square(Q_X + KD - 1, tile(xT, KD - 1))
            split_hi(4, 0, fresh=True)
            act.preload_act_table_set("natural_log")
            inv_rms(N_X, rs[:, :], D)
            split_hi(5, 1, fresh=True)
            act.wait_ge(pool_const, 4)
            act.activation(neg_tri[:, :], scratch[:, :], ACT.Copy).then_inc(const_r, 1)
            act.activation(neg_ones[:, :], ones[:, :], ACT.Copy, scale=-1.0).then_inc(const_r, 1)
            for n in range(2):
                act.wait_ge(evac, n + 1)
                square(Q_CQ + n, tile(c_raw, n))
            act.wait_ge(evac, 3)
            act.activation(sq_kv[:, :], c_raw[:, 2, :], ACT.Square).then_inc(sq_kv_ok, 1)
            act.wait_ge(trig_arg, 1)
            r = slice(NOPE, QK)
            act.activation(sin_t[r, :], ang[r, :], ACT.Sin).then_inc(trig_ok, 1)
            act.activation(cos_t[r, :], turns[r, :], ACT.Sin, bias=half_pi_c[r, :]).then_inc(trig_ok, 1)
            act.wait_ge(wu_in, 32)
            act.activation(wu_hi[:, :], wu_raw[:, :], ACT.Copy).then_inc(wu_hi_ok, 1)
            split_hi(6, 0)
            act.preload_act_table_set("natural_log")
            for n, size, b in ((0, QR, 7), (1, KVR, 6)):
                act.wait_ge(stat_ok, N_CQ + n + 1)
                act.activation(rs_c[n][:, :], ps[b][:, :], ACT.Ln, scale=1.0 / size, bias=eps_c).then_inc(ln_ok, 1)
            exp_and_ln()
            for n in range(2):
                act.wait_ge(ln_ok, N_CQ + n + 1)
                act.activation(rs_c[n][:, :], rs_c[n][:, :], ACT.Exp, scale=-0.5).then_inc(rs_ok, 1)
            act.wait_ge(kr_ok, 1)
            act.wait_ge(unit_done, 4)
            for b in range(2):
                act.activation(k_hi[b][r, :], roped[r, :], ACT.Copy).then_inc(kr_hi_ok, 1)
            for n in range(3):
                act.wait_ge(cn_ok, n + 1)
                dst = cq_hi[:, n, :] if n < 2 else ckv_hi[:, :]
                act.activation(dst, c_norm[:, n, :], ACT.Copy).then_inc(c_hi_ok, 1)
            split_hi(7, 1)
            for t in range(NT):
                act.wait_ge(va_mm, t + 1)
                act.activation(va_hi[:, t, :], ps[VA_BANK[t]][:, :], ACT.Copy).then_inc(va_hi_ok, 1)
            def stage_hi(h):
                b = h % 2
                act.wait_ge(proj_mm, 2 * h + 1)
                if h >= 2:
                    act.wait_ge(s_mm, 3 * (h - 1))
                act.activation(q_hi[b][0:NOPE, :], ps[4][0:NOPE, :], ACT.Copy).then_inc(qk_hi_ok, 1)
                act.wait_ge(proj_mm, 2 * h + 2)
                act.activation(k_hi[b][0:NOPE, :], ps[5][0:NOPE, :], ACT.Copy).then_inc(qk_hi_ok, 1)

            def stage_rope_hi(h):
                act.wait_ge(rope_ok, h + 1)
                act.activation(q_hi[h % 2][r, :], roped[r, :], ACT.Copy).then_inc(qk_hi_ok, 1)

            def mla_out(h):
                act.wait_ge(pv_mm, h + 1)
                rows = slice(h % 2 * DV, (h % 2 + 1) * DV)
                act.activation(oa[rows, h // 2, :], ps[6][rows, :], ACT.Copy).then_inc(o_ok, 1)

            def sb_stage_hi(h):
                rows = slice(h % 2 * SBD, (h % 2 + 1) * SBD)
                if h >= 2:
                    act.wait_ge(z_mm, 4 * (h - 1))
                act.activation(k_st[h % 2][rows, :], sbk[rows, h // 2, :], ACT.Copy).then_inc(qk_b_hi_ok, 1)
                act.activation(qq_hi[h % 2][rows, :], sbq[rows, h // 2, :], ACT.Copy).then_inc(qk_b_hi_ok, 1)

            stage_hi(0)
            split_hi(8, 0)
            stage_rope_hi(0)
            for h in range(NH):
                for i in range(NT):
                    p = probs[:, P_AT[i]:P_AT[i] + (i + 1) * P]
                    act.wait_ge(s_ok, 4 * h + i + 1)
                    act.activation(p, p, ACT.Exp, bias=stat[:, i:i + 1], scale=-1.0,
                                   accum_out=stat[:, 8 + i:9 + i]).then_inc(e_ok, 1)
                if h + 1 < NH:
                    stage_hi(h + 1)
                else:
                    sb_stage_hi(0)
                act.wait_ge(r_ok, h + 1)
                act.wait_ge(e_ok, 4 * h + 4)
                for i in range(NT):
                    p = probs[:, P_AT[i]:P_AT[i] + (i + 1) * P]
                    act.activation(p, p, ACT.Copy, scale=stat[:, 12 + i:13 + i]).then_inc(p_ok, 1)
                if h >= 1:
                    mla_out(h - 1)
                split_hi(fills[h][-1] + 1, (fills[h][-1] + 1) % 2)
                if h + 1 < NH:
                    stage_rope_hi(h + 1)
                for i in range(NT):
                    act.wait_ge(t_mm, 3 * h + DONE[i])
                    if h >= 1 and i == 0:
                        act.wait_ge(pv_mm, h)
                    dst = pT[:, i * P:i * P + (i + 1) * PT_STEP].rearrange("p (j c) -> p j c", c=PT_STEP)[:, :, 0:P]
                    src = ps[T_BANK[i]][:, T_COL[i]:T_COL[i] + (i + 1) * P].rearrange("p (a n) -> p a n", a=i + 1)
                    act.activation(dst, src, ACT.Copy).then_inc(pt_hi_ok, 1)

            def softplus(h):
                for n, j in enumerate((3, 2, 1, 0)):
                    st = stick[:, S_AT[j]:S_AT[j] + S - j * P]
                    act.wait_ge(z_ok, 4 * h + n + 1)
                    if h >= 1:
                        act.wait_ge(a_lo_ok, 4 * (h - 1) + n + 1)
                    d0 = j * P - Q0[j]
                    steps.link(act.activation(st, ps[5 - j][:, d0:d0 + S - j * P], ACT.Abs))
                    steps.link(act.activation(st, st, ACT.Exp, scale=-1.0))
                    act.activation(st, st, ACT.Ln, bias=one_c).then_inc(l_ok, 1)

            def softplus_hi(h):
                for n, j in enumerate((3, 2, 1, 0)):
                    w = S - j * P
                    act.wait_ge(sp_ok, 4 * h + n + 1)
                    if h >= 1 and n == 0:
                        act.wait_ge(w_mm, 4 * h)
                    d = OFF[j] + j * P - Q0[j]
                    act.activation(sp_hi[:, d:d + w], stick[:, S_AT[j]:S_AT[j] + w], ACT.Copy).then_inc(sp_hi_ok, 1)

            def v_hi(tiles):
                for t in tiles:
                    act.wait_ge(vT_mm, t + 1)
                    act.activation(vb_hi[:, t, :], ps[V_BANK[t % 2]][:, :], ACT.Copy).then_inc(vb_hi_ok, 1)

            softplus(0)
            v_hi((0, 1))
            softplus_hi(0)
            split_hi(U_GATE + 1, 1)
            mla_out(NH - 1)
            v_hi((2, 3))

            def sb_out(h):
                act.wait_ge(pvb_mm, h + 1)
                rows = slice(h % 2 * SBD, (h % 2 + 1) * SBD)
                act.activation(ob_hi[rows, h // 2, :], ps[6][rows, :], ACT.Copy).then_inc(ob_hi_ok, 1)

            def mla_out_hi(half):
                t = 2 * half
                act.activation(oa_hi[:, t:t + 2, :], oa[:, t:t + 2, :], ACT.Copy).then_inc(oa_hi_ok, 1)

            for h in range(SBH):
                if h >= 1:
                    softplus(h)
                    softplus_hi(h)
                if h >= 1:
                    u = U_GATE + 2 * h
                    split_hi(u + 1, (u + 1) % 2)
                    sb_out(h - 1)
                if h + 1 < SBH:
                    sb_stage_hi(h + 1)
                if h == SBH - 1:
                    act.wait_ge(qk_b_lo_ok, 4 * SBH)
                    mla_out_hi(1)
                for n, j in enumerate((3, 2, 1, 0)):
                    w = S - j * P
                    act.wait_ge(w_mm, 4 * h + n + 1)
                    act.wait_ge(sp_lo_ok, 4 * h + n + 1)
                    d0 = j * P - Q0[j]
                    act.activation(stick[:, S_AT[j]:S_AT[j] + w], ps[5 - j][:, d0:d0 + w], ACT.Exp).then_inc(a_ok, 1)
                for n, j in enumerate((3, 2, 1, 0)):
                    w = S - j * P
                    act.wait_ge(a_ok, 4 * h + n + 1)
                    if h >= 1 and n == 0:
                        act.wait_ge(pvb_mm, h)
                    d = OFF[j] + j * P - Q0[j]
                    act.activation(a_hi[:, d:d + w], stick[:, S_AT[j]:S_AT[j] + w], ACT.Copy).then_inc(a_hi_ok, 1)
                u = U_GATE + 2 * h + 1
                split_hi(u + 1, (u + 1) % 2)
                if h == SBH - 2:
                    act.wait_ge(qk_b_lo_ok, 4 * 4)
                    mla_out_hi(0)
            split_hi(U_MERGE + 1, 1)
            act.preload_act_table_set("sigmoid_and_others")
            sb_out(SBH - 1)
            act.wait_ge(evac, G_MERGE)

            def merge(t):
                for part in range(2):
                    for b in range(2):
                        g = tile(gates, 8 * part + 2 * t + b)
                        act.activation(g, g, ACT.Sigmoid, bias=col(gains, R_BIAS + 8 * part + 2 * t + b)).then_inc(sig_ok, 1)
                    split_hi(U_MERGE + 2 * t + 2 + part, part)
                for b in range(2):
                    act.wait_ge(m_ok, 2 * t + b + 1)
                    act.activation(tile(m_hi, 2 * t + b), tile(gates, 2 * t + b), ACT.Copy).then_inc(m_hi_ok, 1)
            repeat(act, 0, 4, merge)

            act.preload_act_table_set("natural_log")
            act.wait_ge(mem_sq, 2)
            steps.link(act.activation(stat_x[:, 4:6], stat_x[:, 4:6], ACT.Ln, scale=1.0 / D, bias=eps_c))
            exp_and_ln()
            act.activation(stat_x[:, 4:6], stat_x[:, 4:6], ACT.Exp, scale=-0.5).then_inc(mem_rs, 1)

            def wo(i):
                for s in range(2):
                    m = 2 * i + s
                    split_hi(U_WO + m + 2, s)
                    act.wait_ge(evac, G_WO + m + 1)
                    square(Q_X2 + m, tile(xT, m))
                    gained(h_hi, m, tile(xT, m), R_X, h_hi_ok)
            wo(0)
            for m in range(KD):
                act.wait_ge(mem_T, m // 2 + 1)
                act.activation(mn_hi[:, m, :], ps[4 + m // 2][:, m % 2 * MEM:(m % 2 + 1) * MEM], ACT.Copy,
                               scale=gains[:, R_MEM + m:R_MEM + m + 1]).then_inc(mn_hi_ok, 1)
                if m == 3:
                    wo(1)
            wo(2)
            act.preload_act_table_set("natural_log")
            wo(3)

            for u in (U_XV + 2, U_XV + 3):
                split_hi(u, u % 2)
            split_hi(U_XKQ, 0)
            inv_rms(N_X2, rs[:, :], D, between=lambda: split_hi(U_XKQ + 1, 1))
            act.wait_ge(unit_done, U_XKQ)
            for t in range(2):
                act.activation(xv_hi[:, t, :], ps[4 + t][:, :], ACT.Copy).then_inc(xv_hi_ok, 1)

            def x_keys(h):
                if h:
                    split_hi(U_XKQ + 2 * h + 1, 1)
                act.wait_ge(unit_done, U_XKQ + 2 * h + 1)
                act.activation(xk_hi[:, h, :], ps[0][:, 0:MEM], ACT.Copy).then_inc(xk_hi_ok, 1)

            def x_queries(h):
                split_hi(U_XKQ + 2 * h + 2, 0)
                act.wait_ge(evac, G_XKQ + 2 * h + 2)
                act.activation(xq_hi[:, h, :], xq_raw[h % 2][:, :], ACT.Copy).then_inc(xq_hi_ok, 1)

            def x_exp(h):
                if h >= 1:
                    act.wait_ge(xp_ok, 4 * h)
                for i in range(NT):
                    act.wait_ge(xs_max, 2 * h + i // 2 + 1)
                    act.activation(xp[h % 2][:, i, :], ps[2 + i // 2][:, i % 2 * MEM:(i % 2 + 1) * MEM], ACT.Exp,
                                   bias=stat_x[:, 8 + i:9 + i], scale=X_SCALE,
                                   accum_out=stat_x[:, 12 + i:13 + i]).then_inc(xe_ok, 1)

            def x_turned(h):
                for j in range(2):
                    act.wait_ge(xt_mm, 2 * h + j + 1)
                    if h >= 1:
                        act.wait_ge(xpv_mm, h)
                    act.activation(xpT_hi[:, j, :], ps[4 + j][:, :], ACT.Copy).then_inc(xt_hi_ok, 1)

            def x_out(h):
                act.wait_ge(xpv_mm, h + 1)
                act.activation(xo_hi[:, h, :], ps[6][:, :], ACT.Copy).then_inc(xo_hi_ok, 1)

            def late_split(n):
                act.wait_ge(raw_in[n], 8 * (U_XO + 2))
                act.wait_ge(unit_done, U_XO - 1)
                act.activation(late_hi[n][:, :], raw[n][:, :], ACT.Copy).then_inc(hi_done, 1)

            x_keys(0)
            x_queries(0)
            x_keys(1)
            for h in range(XH):
                x_exp(h)
                if h + 1 < XH:
                    x_queries(h + 1)
                else:
                    late_split(0)
                x_turned(h)
                if h + 2 < XH:
                    x_keys(h + 2)
                elif h + 2 == XH:
                    split_hi(U_XO + 1, 1)
                x_out(h)

            late_split(1)
            act.preload_act_table_set("natural_log")

            def normed_hi(m):
                act.wait_ge(evac, G_XO + m + 1)
                gained(h_hi, m, tile(xT, m), R_FFN, h_hi_ok)

            def normed_square(m):
                square(Q_X3 + m, tile(xT, m))

            normed_hi(0)
            normed_square(0)
            normed_hi(1)
            split_hi(U_FFN, 0, used=U_XO + 1)
            normed_hi(2)
            normed_square(1)
            normed_hi(3)
            normed_square(2)
            split_hi(U_FFN + 1, 1, used=U_XO + 2)
            normed_hi(4)
            normed_square(3)
            normed_hi(5)
            normed_square(4)
            normed_hi(6)
            normed_hi(7)
            normed_square(5)
            split_hi(U_FFN + 2, 0)
            normed_square(6)
            normed_square(7)
            inv_rms(N_X3, rs[:, :], D, between=lambda: split_hi(U_FFN + 3, 1))

            def ffn(i, head=False):
                for b in range(2):
                    m = 2 * i + b
                    if not head:
                        split_hi(U_FFN + 2 * m + 1, 1)
                    if not (head and b == 0):
                        split_hi(U_FFN + 2 * m + 2, 0)
                    act.wait_ge(evac, G_FFN + 2 * m + 1)
                    act.activation(g_t[b][:, :], g_t[b][:, :], ACT.Silu).then_inc(silu_ok, 1)
                    act.wait_ge(f_ok, m + 1)
                    act.activation(tile(f_hi, m), u_t[b][:, :].rearrange("p (a n) -> p a n", a=1), ACT.Copy).then_inc(f_hi_ok, 1)
            ffn(0, head=True)
            repeat(act, 1, KF // 2 - 1, ffn)

            for m in range(KD):
                if m == 1:
                    act.preload_act_table_set("sqrt_and_others")
                for j in range(3):
                    u = U_DOWN + 3 * m + j + 1
                    if u < U_END - 1:
                        split_hi(u, u % 2, P * DOWN_K[(j + 1) % 3])
                    elif u == U_END - 1:
                        act.wait_ge(raw_in[1], 8 * (u - 1))
                        act.activation(end_hi[:, 0:P * DOWN_K[2]], raw[1][:, 0:P * DOWN_K[2]], ACT.Copy).then_inc(hi_done, 1)
                    if m >= 1 and j == 0:
                        act.wait_ge(evac, G_DOWN + m)
                        act.activation(yT[:, (m - 1) % 4, :], xT[:, m - 1, :], ACT.Copy,
                                       scale=gains[:, R_FINAL + m - 1:R_FINAL + m]).then_inc(y_ok, 1)
                        square(Q_X4 + m - 1, tile(xT, m - 1))
                    if m == 4 and j == 1:
                        act.wait_ge(yT_mm, 1)
                        for t in range(NT):
                            act.activation(y_nat[:, t, 0:S], ps[2 + t][:, :], ACT.Copy).then_inc(y_ok, 1)
            act.wait_ge(sq_added, Q_X4 + KD - 1)
            for half in range(2):
                c, tiles = slice(half * MEM, (half + 1) * MEM), slice(2 * half, 2 * half + 2)
                act.wait_ge(end_ok, half + 1)
                act.activation(sq_tile[:, c], xT[:, KD - 1, c], ACT.Square).then_inc(sq_ok, 1)
                act.wait_ge(stat_ok, N_X4 + half + 1)
                act.activation(stat[:, tiles], ps[7][:, tiles], ACT.Sqrt, scale=1.0 / D, bias=eps_c).then_inc(rs_ok, 1)
                act.wait_ge(y_rs, half + 1)
                act.wait_ge(yT_mm, half + 2)
                for t in (2 * half, 2 * half + 1):
                    act.activation(y_nat[:, t, S:D], ps[2 + t][:, :], ACT.Copy, scale=stat[:, 4 + t:5 + t]).then_inc(y_right, 1)

        @block.gpsimd
        def _(pool):
            steps = Steps(pool, pool_step)
            steps.link(pool.memset(ident[:, :], 0.0))
            pool.affine_select(out=ident[:, :], in_=ident[:, :], compare_op=ALU.not_equal, fill=1.0, base=0,
                               pattern=[[-1, P]], channel_multiplier=1).then_inc(pool_const, 1)
            pool.dma_start(pos_i[NOPE:QK, :], positions[0:1, :].to_broadcast([ROPE, S])).then_inc(pos_in, 16)
            pool.dma_start(consts[NOPE:QK, 3:4], signed_freq).then_inc(freq_in, 16)
            pool.memset(ones[:, :], 1.0).then_inc(pool_const, 1)
            steps.link(pool.memset(scratch[:, :], -1.0))
            pool.affine_select(out=scratch[:, :], in_=scratch[:, :], compare_op=ALU.is_ge, fill=0.0, base=0,
                               pattern=[[-1, P]], channel_multiplier=1).then_inc(pool_const, 1)
            pool.memset(consts[:, 0:1], EPS)
            pool.memset(consts[:, 1:2], HALF_PI)
            pool.memset(consts[:, 2:3], 1.0).then_inc(pool_const, 1)
            pool.memset(mask_row[:, 0:384], 0.0)
            steps.link(pool.memset(mask_row[:, 384:512], 0.0))
            pool.affine_select(out=mask_row[:, 384:512], in_=mask_row[:, 384:512], compare_op=ALU.is_ge, fill=NEG,
                               base=0, pattern=[[-1, P]], channel_multiplier=1).then_inc(pool_const, 1)
            steps.link(pool.memset(mask_kq[:, :], 0.0))
            pool.affine_select(out=mask_kq[:, :], in_=mask_kq[:, :], compare_op=ALU.is_gt, fill=NEG,
                               base=0, pattern=[[1, P]], channel_multiplier=-1).then_inc(pool_const, 1)
            pool.memset(sq_sum[:, :], 0.0).then_inc(sum_clear, 1)

            def add_squares(q0, count, clears, n_stat):
                pool.wait_ge(sum_clear, clears)

                def one(m):
                    pool.wait_ge(sq_ok, q0 + m + 1)
                    if q0 or not isinstance(m, int) or m:
                        pool.wait_ge(sq_added, q0 + m)
                    pool.tensor_tensor(sq_sum[:, :], sq_sum[:, :], sq_tile[:, :], ALU.add).then_inc(sq_added, 1)
                if q0 >= Q_X2:
                    repeat(pool, 0, count, one)
                else:
                    for m in range(count):
                        one(m)
                if n_stat < N_X4:
                    pool.wait_ge(stat_ok, n_stat + 1)
                    pool.memset(sq_sum[:, :], 0.0).then_inc(sum_clear, 1)

            add_squares(Q_X, KD, 1, N_X)
            add_squares(Q_CQ, 2, 2, N_CQ)
            for h in range(NH):
                pool.wait_ge(dve_rope, 2 * h + 2)
                if h:
                    pool.wait_ge(rope_ok, h)
                else:
                    pool.wait_ge(sum_clear, 3)
                r = slice(NOPE, QK)
                steps.link(pool.tensor_tensor(swapped[r, :], swapped[r, :], sin_t[r, :], ALU.mult))
                pool.tensor_tensor(roped[r, :], roped[r, :], swapped[r, :], ALU.add).then_inc(rope_ok, 1)
            pool.wait_ge(rope_ok, NH)
            for parts, used, count, own, step in (((sp_hi, sp_lo), s_mm, 3 * NH, rope_ok, NH), ((a_hi, a_lo), pv_mm, NH, sp_zero_ok, 1)):
                pool.wait_ge(used, count)
                pool.wait_ge(own, step)
                for part in parts:
                    last = pool.memset(part[:, OFF[3]:OFF[3] + P].bitcast(mybir.dt.uint32), 0)
                last.then_inc(sp_zero_ok, 1)
            pool.wait_ge(z_mm, 4 * SBH)
            pool.dma_start(mem_nat[:, :, :], mem[0].rearrange("(t p) d -> p t d", p=P)).then_inc(mem_in, 16)
            pool.wait_ge(mem_in, 16)
            for t in range(2):
                steps.link(pool.tensor_tensor(mem_junk[:, :], mem_nat[:, t, :], mem_nat[:, t, :], ALU.mult))
                w = D // 2
                while w > 1:
                    steps.link(pool.tensor_tensor(mem_junk[:, 0:w], mem_junk[:, 0:w], mem_junk[:, w:2 * w], ALU.add))
                    w //= 2
                pool.tensor_tensor(stat_x[:, 4 + t:5 + t], mem_junk[:, 0:1], mem_junk[:, 1:2], ALU.add).then_inc(mem_sq, 1)
                pool.wait_ge(mem_sq, t + 1)
            add_squares(Q_X2, KD, 3, N_X2)
            add_squares(Q_X3, KD, 4, N_X3)
            add_squares(Q_X4, KD - 1, 5, N_X4)

        @block.vector
        def _(dve):
            steps = Steps(dve, dve_step)

            def split_lo(u, s, n=1024):
                dve.wait_ge(hi_done, u + 1)
                dve.tensor_tensor(w_lo[s][:, 0:n], raw[s][:, 0:n], fl(w_hi[s][:, 0:n]), ALU.subtract).then_inc(lo_done, 1)

            def gained_lo(m, row, count):
                dve.wait_ge(h_hi_ok, count)
                dve.scalar_tensor_tensor(out=tile(h_lo, m), in0=tile(xT, m), scalar=col(gains, row + m),
                                         in1=fl(tile(h_hi, m)), op0=ALU.mult, op1=ALU.subtract).then_inc(h_lo_ok, 1)

            r = slice(NOPE, QK)

            def split_first(n):
                w = KD * (QK if n == 3 else P)
                dve.wait_ge(hi_done, n + 1)
                dve.tensor_tensor(first_lo[n][:, 0:w], (raw + raw_more)[n][:, 0:w], fl(first_hi[n][:, 0:w]), ALU.subtract).then_inc(lo_done, 1)

            c1, c2 = 6.28125, 0.0019350051879882812
            c3 = float(2 * np.pi - c1 - c2)
            magic = 1.5 * 2.0 ** 23

            def reduce_angles(unit):
                steps.link(dve.tensor_scalar(turns[r, :], ang[r, :], 1.0 / (2 * np.pi * unit), magic, ALU.mult, ALU.add))
                steps.link(dve.tensor_scalar(turns[r, :], turns[r, :], magic, unit, ALU.subtract, ALU.mult))
                for c in (c1, c2, c3):
                    steps.link(dve.scalar_tensor_tensor(out=ang[r, :], in0=turns[r, :], scalar=-c, in1=ang[r, :],
                                                        op0=ALU.mult, op1=ALU.add))
            dve.wait_ge(gains_T, 1)
            dve.tensor_copy(gains[:, 0:8], ps[7][:, 0:8]).then_inc(gains_ok, 1)
            split_first(0)

            def x_keep(m):
                dve.wait_ge(x_T, m + 1)
                dve.tensor_copy(tile(xT, m), bank(4 + m % 3)).then_inc(x_kept, 1)

            x_keep(0)
            for m in range(KD):
                if m + 1 < KD:
                    x_keep(m + 1)
                gained_lo(m, R_MIX, m + 1)
                if m - 1 in FIRST_HI:
                    split_first(FIRST_HI.index(m - 1) + 1)
            dve.wait_ge(pos_in, 16)
            dve.wait_ge(freq_in, 16)
            steps.link(dve.tensor_copy(turns[r, :], pos_i[r, :]))
            steps.link(dve.tensor_scalar(ang[r, :], turns[r, :], consts[r, 3:4], None, ALU.mult))
            reduce_angles(4096.0)
            split_lo(4, 0)
            reduce_angles(1.0)
            pi32 = 3.1415925
            steps.link(dve.tensor_scalar(ang[r, :], ang[r, :], pi32, -pi32, ALU.min, ALU.max))
            dve.scalar_tensor_tensor(out=turns[r, :], in0=ang[r, :], scalar=-1.0, in1=ang[r, :], op0=ALU.mult,
                                     op1=ALU.min).then_inc(trig_arg, 1)
            dve.wait_ge(gains_T, 2)
            dve.tensor_copy(gains[:, 8:R_ALL], ps[6][:, 8:R_ALL]).then_inc(gains_ok, 1)
            dve.wait_ge(rs_ok, 1)
            for n in range(3):
                if n == 2:
                    split_lo(5, 1)
                dve.wait_ge(unit_done, n + 1)
                dve.tensor_tensor(c_raw[:, n, :], ps[n][:, :], rs[:, :], ALU.mult).then_inc(evac, 1)
            dve.wait_ge(unit_done, 4)
            dve.tensor_tensor(c_raw[r, 3, :], ps[3][r, :], rs[r, :], ALU.mult).then_inc(evac, 1)
            dve.wait_ge(evac, 4)
            dve.wait_ge(trig_ok, 2)
            swap = list(range(ROPE // 2, ROPE)) + list(range(ROPE // 2))
            steps.link(dve.stream_shuffle(swapped[r, :], c_raw[r, 3, :], swap))
            steps.link(dve.tensor_tensor(swapped[r, :], swapped[r, :], sin_t[r, :], ALU.mult))
            steps.link(dve.tensor_tensor(roped[r, :], c_raw[r, 3, :], cos_t[r, :], ALU.mult))
            dve.tensor_tensor(roped[r, :], roped[r, :], swapped[r, :], ALU.add).then_inc(kr_ok, 1)

            def sb_epilogue(u):
                n = u - U_SB
                dve.wait_ge(unit_done, u + 1)
                dst = (sbq, sbk, sbvT)[n // 4][:, n % 4, :]
                b = u if u in (4, 5) else u % 2
                dve.scalar_tensor_tensor(out=dst, in0=ps[b][:, :], scalar=SB_SCALE if n < 4 else 1.0,
                                         in1=rs[:, :], op0=ALU.mult, op1=ALU.mult).then_inc(evac, 1)

            def gate_epilogue(u):
                dve.wait_ge(unit_done, u + 1)
                dve.tensor_tensor(gates[:, u - U_GATE, :], ps[u % 2][:, :], rs[:, :], ALU.mult).then_inc(evac, 1)

            split_lo(6, 0)
            dve.wait_ge(wu_hi_ok, 1)
            dve.tensor_tensor(wu_lo[:, :], wu_raw[:, :], fl(wu_hi[:, :]), ALU.subtract).then_inc(wu_lo_ok, 1)
            for n in range(3):
                row, which = (R_Q, R_Q + 1, R_KV)[n], (0, 0, 1)[n]
                dve.wait_ge(rs_ok, 2 + which)
                dve.scalar_tensor_tensor(out=c_norm[:, n, :], in0=c_raw[:, n, :], scalar=gains[:, row:row + 1],
                                         in1=rs_c[which][:, :], op0=ALU.mult, op1=ALU.mult).then_inc(cn_ok, 1)
            for n in range(3):
                dst, hi = ((cq_lo, cq_hi) if n < 2 else (ckv_lo, ckv_hi))
                dst, hi = (dst[:, n, :], hi[:, n, :]) if n < 2 else (dst[:, :], hi[:, :])
                dve.wait_ge(c_hi_ok, n + 1)
                dve.tensor_tensor(dst, c_norm[:, n, :], fl(hi), ALU.subtract).then_inc(c_lo_ok, 1)
            for b in range(2):
                dve.wait_ge(kr_hi_ok, b + 1)
                dve.tensor_tensor(k_lo[b][r, :], roped[r, :], fl(k_hi[b][r, :]), ALU.subtract).then_inc(kr_lo_ok, 1)
            dve.wait_ge(sq_kv_ok, 1)
            sb_epilogue(4)
            sb_epilogue(5)
            split_lo(7, 1)
            for t in range(NT):
                dve.wait_ge(va_hi_ok, t + 1)
                dve.tensor_tensor(va_lo[:, t, :], ps[VA_BANK[t]][:, :], fl(va_hi[:, t, :]), ALU.subtract).then_inc(va_lo_ok, 1)

            def stage_lo(h):
                b = h % 2
                dve.wait_ge(proj_mm, 2 * h + 1)
                if h >= 1:
                    dve.wait_ge(rope_lo_ok, h)
                else:
                    dve.wait_ge(kr_lo_ok, 2)
                dve.wait_ge(qk_hi_ok, 3 * h + 1)
                dve.stream_shuffle(swapped[r, :], ps[4][r, :], swap).then_inc(dve_rope, 1)
                dve.tensor_tensor(roped[r, :], ps[4][r, :], cos_t[r, :], ALU.mult).then_inc(dve_rope, 1)
                dve.tensor_tensor(q_lo[b][0:NOPE, :], ps[4][0:NOPE, :], fl(q_hi[b][0:NOPE, :]), ALU.subtract).then_inc(qk_lo_ok, 1)
                dve.wait_ge(qk_hi_ok, 3 * h + 2)
                dve.tensor_tensor(k_lo[b][0:NOPE, :], ps[5][0:NOPE, :], fl(k_hi[b][0:NOPE, :]), ALU.subtract).then_inc(qk_lo_ok, 1)

            def stage_rope_lo(h):
                dve.wait_ge(qk_hi_ok, 3 * h + 3)
                dve.tensor_tensor(q_lo[h % 2][r, :], roped[r, :], fl(q_hi[h % 2][r, :]), ALU.subtract).then_inc(rope_lo_ok, 1)

            def sb_stage_lo(h):
                b, p = h % 2, h // 2
                rows, other = (slice(x * SBD, (x + 1) * SBD) for x in (b, 1 - b))
                dve.wait_ge(qk_b_hi_ok, 2 * h + 1)
                dve.tensor_tensor(k_st[b][other, :], sbk[rows, p, :], fl(k_st[b][rows, :]), ALU.subtract).then_inc(qk_b_lo_ok, 1)
                dve.wait_ge(qk_b_hi_ok, 2 * h + 2)
                dve.tensor_tensor(qq_lo[b][rows, :], sbq[rows, p, :], fl(qq_hi[b][rows, :]), ALU.subtract).then_inc(qk_b_lo_ok, 1)
                dve.tensor_copy(qq_hi[b][other, :], qq_hi[b][rows, :]).then_inc(qk_b_lo_ok, 1)
                dve.wait_ge(qk_b_lo_ok, 4 * h + 2)
                dve.tensor_copy(qq_lo[b][other, :], qq_lo[b][rows, :]).then_inc(qk_b_lo_ok, 1)

            def sb_mask(h):
                for n, j in enumerate((3, 2, 1, 0)):
                    d0 = j * P - Q0[j]
                    dve.wait_ge(z_mm, 4 * h + n + 1)
                    dve.tensor_tensor(ps[5 - j][:, d0:d0 + P], ps[5 - j][:, d0:d0 + P], mask_kq[:, :], ALU.add).then_inc(z_ok, 1)

            def sb_softplus(h):
                for n, j in enumerate((3, 2, 1, 0)):
                    w, d0 = S - j * P, j * P - Q0[j]
                    st = stick[:, S_AT[j]:S_AT[j] + w]
                    dve.wait_ge(l_ok, 4 * h + n + 1)
                    dve.scalar_tensor_tensor(out=st, in0=ps[5 - j][:, d0:d0 + w], scalar=0.0, in1=st,
                                             op0=ALU.max, op1=ALU.add).then_inc(sp_ok, 1)

            def sb_softplus_lo(h):
                for n, j in enumerate((3, 2, 1, 0)):
                    w = S - j * P
                    d = OFF[j] + j * P - Q0[j]
                    dve.wait_ge(sp_hi_ok, 4 * h + n + 1)
                    dve.tensor_tensor(sp_lo[:, d:d + w], stick[:, S_AT[j]:S_AT[j] + w], fl(sp_hi[:, d:d + w]), ALU.subtract).then_inc(sp_lo_ok, 1)

            def sb_out_lo(h):
                rows = slice(h % 2 * SBD, (h % 2 + 1) * SBD)
                dve.wait_ge(ob_hi_ok, h + 1)
                dve.tensor_tensor(ob_lo[rows, h // 2, :], ps[6][rows, :], fl(ob_hi[rows, h // 2, :]), ALU.subtract).then_inc(ob_ok, 1)

            dve.wait_ge(pool_const, 6)
            stage_lo(0)
            split_lo(8, 0)
            sb_epilogue(6)
            stage_rope_lo(0)
            sb_epilogue(7)
            dve.wait_ge(const_r, 2)
            dve.wait_ge(c_hi_ok, 3)
            for base in (0, 1664):
                dve.memset(pT[:, base + 3 * PT_STEP + 256:base + 3 * PT_STEP + 384].bitcast(mybir.dt.uint32), 0).then_inc(pt_zero_ok, 1)
            for h in range(NH):
                for i in range(NT):
                    w = (i + 1) * P
                    dve.wait_ge(s_mm, 3 * h + DONE[i])
                    if h >= 1 and i == 0:
                        dve.wait_ge(t_mm, 3 * h)
                    dve.tensor_tensor_reduce(out=probs[:, P_AT[i]:P_AT[i] + w], in0=ps[S_BANK[i]][:, S_COL[i]:S_COL[i] + w],
                                             in1=mask_row[:, S - w:S], scale=-MLA_SCALE, scalar=3.0e38,
                                             op0=ALU.add, op1=ALU.min, accum_out=stat[:, i:i + 1]).then_inc(s_ok, 1)
                dve.wait_ge(e_ok, 4 * h + 4)
                dve.reciprocal(stat[:, 12:16], stat[:, 8:12]).then_inc(r_ok, 1)
                if h + 1 < NH:
                    stage_lo(h + 1)
                else:
                    sb_stage_lo(0)
                u = fills[h][-1]
                split_lo(u + 1, (u + 1) % 2)
                if h + 1 < NH:
                    stage_rope_lo(h + 1)
                if h + 1 == NH:
                    sb_epilogue(u)
                for i in range(NT):
                    dve.wait_ge(pt_hi_ok, 4 * h + max(i + 1, 2))
                    v = slice(i * P, i * P + (i + 1) * PT_STEP)
                    hi = pT[:, v].rearrange("p (j c) -> p j c", c=PT_STEP)[:, :, 0:P]
                    lo = pT[:, 1664 + v.start:1664 + v.stop].rearrange("p (j c) -> p j c", c=PT_STEP)[:, :, 0:P]
                    src = ps[T_BANK[i]][:, T_COL[i]:T_COL[i] + (i + 1) * P].rearrange("p (a n) -> p a n", a=i + 1)
                    dve.tensor_tensor(lo, src, fl(hi), ALU.subtract).then_inc(pt_lo_ok, 1)
                if h + 1 < NH:
                    sb_epilogue(u)
            def v_lo(tiles):
                for t in tiles:
                    dve.wait_ge(vb_hi_ok, t + 1)
                    dve.tensor_tensor(vb_lo[:, t, :], ps[V_BANK[t % 2]][:, :], fl(vb_hi[:, t, :]), ALU.subtract).then_inc(vb_lo_ok, 1)

            sb_mask(0)
            sb_softplus(0)
            v_lo((0, 1))
            sb_softplus_lo(0)
            split_lo(U_GATE + 1, 1)
            v_lo((2,))
            dve.wait_ge(o_ok, NH)
            gate_epilogue(U_GATE)
            v_lo((3,))

            def mla_out_lo(half):
                t = 2 * half
                dve.wait_ge(oa_hi_ok, half + 1)
                dve.tensor_tensor(oa_lo[:, t:t + 2, :], oa[:, t:t + 2, :], fl(oa_hi[:, t:t + 2, :]), ALU.subtract).then_inc(oa_lo_ok, 1)

            for h in range(SBH):
                if h >= 1:
                    sb_mask(h)
                    if h == SBH - 1:
                        mla_out_lo(0)
                    sb_softplus(h)
                    sb_softplus_lo(h)
                if h >= 1:
                    u = U_GATE + 2 * h
                    split_lo(u + 1, (u + 1) % 2)
                    sb_out_lo(h - 1)
                    gate_epilogue(u)
                if h + 1 < SBH:
                    sb_stage_lo(h + 1)
                if h == SBH - 1:
                    mla_out_lo(1)
                for n, j in enumerate((3, 2, 1, 0)):
                    w = S - j * P
                    d = OFF[j] + j * P - Q0[j]
                    dve.wait_ge(a_hi_ok, 4 * h + n + 1)
                    dve.tensor_tensor(a_lo[:, d:d + w], stick[:, S_AT[j]:S_AT[j] + w], fl(a_hi[:, d:d + w]), ALU.subtract).then_inc(a_lo_ok, 1)
                u = U_GATE + 2 * h + 1
                split_lo(u + 1, (u + 1) % 2)
                gate_epilogue(u)
            split_lo(U_MERGE + 1, 1)
            sb_out_lo(SBH - 1)

            def merge(t):
                for part in range(2):
                    dve.wait_ge(unit_done, U_MERGE + 2 * t + 1 + part)
                    dve.wait_ge(sig_ok, 4 * t + 2 + 2 * part)
                    for b in range(2):
                        g = tile(gates, 8 * part + 2 * t + b)
                        dve.tensor_tensor(g, bank(2 * part + b), g, ALU.mult).then_inc(evac, 1)
                    split_lo(U_MERGE + 2 * t + 2 + part, part)
                for b in range(2):
                    dve.wait_ge(evac, G_MERGE + 4 * t + 3 + b)
                    dve.tensor_tensor(tile(gates, 2 * t + b), tile(gates, 2 * t + b), tile(gates, 8 + 2 * t + b), ALU.add).then_inc(m_ok, 1)
                for b in range(2):
                    dve.wait_ge(m_hi_ok, 2 * t + b + 1)
                    dve.tensor_tensor(tile(m_lo, 2 * t + b), tile(gates, 2 * t + b), fl(tile(m_hi, 2 * t + b)), ALU.subtract).then_inc(m_lo_ok, 1)
            repeat(dve, 0, 4, merge)

            def residual(m, b):
                dve.tensor_tensor(tile(xT, m), bank(b), tile(xT, m), ALU.add).then_inc(evac, 1)

            dve.wait_ge(mem_rs, 1)
            for t in range(2):
                dve.tensor_scalar(mem_nat[:, t, :], mem_nat[:, t, :], stat_x[:, 4 + t:5 + t], None, ALU.mult).then_inc(mem_n, 1)

            def wo(i):
                for s in range(2):
                    m = 2 * i + s
                    dve.wait_ge(unit_done, U_WO + m + 1)
                    residual(m, s)
                    split_lo(U_WO + m + 2, s)
                    gained_lo(m, R_X, KD + m + 1)
            wo(0)
            for m in range(KD):
                dve.wait_ge(mn_hi_ok, m // 2 * 2 + 2)
                dve.scalar_tensor_tensor(out=mn_lo[:, m, :], in0=ps[4 + m // 2][:, m % 2 * MEM:(m % 2 + 1) * MEM],
                                         scalar=gains[:, R_MEM + m:R_MEM + m + 1],
                                         in1=fl(mn_hi[:, m, :]), op0=ALU.mult, op1=ALU.subtract).then_inc(mn_lo_ok, 1)
                if m == 3:
                    wo(1)
            repeat(dve, 2, 2, wo)

            for u in (U_XV + 2, U_XV + 3, U_XKQ, U_XKQ + 1):
                split_lo(u, u % 2)
            for t in range(2):
                dve.wait_ge(xv_hi_ok, t + 1)
                dve.tensor_tensor(xv_lo[:, t, :], ps[4 + t][:, :], fl(xv_hi[:, t, :]), ALU.subtract).then_inc(xv_lo_ok, 1)
            dve.wait_ge(rs_ok, N_X2 + 1)

            def x_keys(h):
                if h:
                    split_lo(U_XKQ + 2 * h + 1, 1)
                dve.wait_ge(xk_hi_ok, h + 1)
                dve.tensor_tensor(xk_lo[:, h, :], ps[0][:, 0:MEM], fl(xk_hi[:, h, :]), ALU.subtract).then_inc(evac, 1)

            def x_queries(h):
                dve.wait_ge(unit_done, U_XKQ + 2 * h + 2)
                dve.tensor_tensor(xq_raw[h % 2][:, :], ps[1][:, :], rs[:, :], ALU.mult).then_inc(evac, 1)
                dve.wait_ge(xq_hi_ok, h + 1)
                dve.tensor_tensor(xq_lo[:, h, :], xq_raw[h % 2][:, :], fl(xq_hi[:, h, :]), ALU.subtract).then_inc(xq_lo_ok, 1)

            def x_softmax(h):
                for c in range(2):
                    dve.wait_ge(xs_mm, 2 * h + c + 1)
                    if h >= 1 and c == 0:
                        dve.wait_ge(xe_ok, 4 * h)
                    steps.link(dve.reduce_max(stat_x[:, 4 + 2 * c:6 + 2 * c], bank(2 + c, 2), AX_X))
                    dve.tensor_scalar(stat_x[:, 8 + 2 * c:10 + 2 * c], stat_x[:, 4 + 2 * c:6 + 2 * c], -X_SCALE, None, ALU.mult).then_inc(xs_max, 1)
                dve.wait_ge(xe_ok, 4 * h + 4)
                steps.link(dve.reciprocal(stat_x[:, 16:20], stat_x[:, 12:16]))
                for i in range(NT):
                    dve.tensor_scalar(xp[h % 2][:, i, :], xp[h % 2][:, i, :], stat_x[:, 16 + i:17 + i], None, ALU.mult).then_inc(xp_ok, 1)
                if h + 1 < XH:
                    split_lo(U_XKQ + 2 * h + 4, 0)

            def late_split(n):
                dve.wait_ge(hi_done, U_XO + 3 + n)
                dve.tensor_tensor(late_lo[n][:, :], raw[n][:, :], fl(late_hi[n][:, :]), ALU.subtract).then_inc(lo_done, 1)

            x_keys(0)
            split_lo(U_XKQ + 2, 0)
            x_queries(0)
            x_keys(1)
            for h in range(XH):
                x_softmax(h)
                if h + 1 < XH:
                    x_queries(h + 1)
                else:
                    late_split(0)
                for j in range(2):
                    dve.wait_ge(xt_hi_ok, 2 * h + j + 1)
                    dve.tensor_tensor(xpT_lo[:, j, :], ps[4 + j][:, :], fl(xpT_hi[:, j, :]), ALU.subtract).then_inc(xt_lo_ok, 1)
                if h + 2 < XH:
                    x_keys(h + 2)
                elif h + 2 == XH:
                    split_lo(U_XO + 1, 1)
                dve.wait_ge(xo_hi_ok, h + 1)
                dve.tensor_tensor(xo_lo[:, h, :], ps[6][:, :], fl(xo_hi[:, h, :]), ALU.subtract).then_inc(xo_lo_ok, 1)

            def xo_residual(v, b):
                dve.wait_ge((xo_mm, unit_done)[b], (v + 1, U_XO + v + 1)[b])
                residual(2 * v + b, XO_BANK[2 * v + b])

            late_split(1)
            for m in range(4):
                xo_residual(m // 2, m % 2)
            for m in range(KD):
                gained_lo(m, R_FFN, 2 * KD + m + 1)
                if m == 1:
                    split_lo(U_FFN, 0)
                    xo_residual(2, 0)
                    xo_residual(2, 1)
                if m == 3:
                    split_lo(U_FFN + 1, 1)
                    xo_residual(3, 0)
                if m == 4:
                    xo_residual(3, 1)
            split_lo(U_FFN + 2, 0)
            split_lo(U_FFN + 3, 1)

            dve.wait_ge(rs_ok, N_X3 + 1)

            def ffn(i, head=False):
                for b in range(2):
                    m = 2 * i + b
                    if not head:
                        split_lo(U_FFN + 2 * m + 1, 1)
                    dve.wait_ge(unit_done, U_FFN + 2 * m + 1)
                    if not head:
                        dve.wait_ge(f_ok, m - 1)
                    dve.tensor_tensor(g_t[b][:, :], ps[2 * b][:, :], rs[:, :], ALU.mult).then_inc(evac, 1)
                    if not (head and b == 0):
                        split_lo(U_FFN + 2 * m + 2, 0)
                    dve.wait_ge(unit_done, U_FFN + 2 * m + 2)
                    if not head:
                        dve.wait_ge(f_lo_ok, m - 1)
                    dve.tensor_tensor(u_t[b][:, :], ps[2 * b + 1][:, :], rs[:, :], ALU.mult).then_inc(evac, 1)
                    dve.wait_ge(silu_ok, m + 1)
                    dve.wait_ge(evac, G_FFN + 2 * m + 2)
                    dve.tensor_tensor(u_t[b][:, :], u_t[b][:, :], g_t[b][:, :], ALU.mult).then_inc(f_ok, 1)
                    dve.wait_ge(f_hi_ok, m + 1)
                    dve.tensor_tensor(tile(f_lo, m), u_t[b][:, :].rearrange("p (a n) -> p a n", a=1), fl(tile(f_hi, m)), ALU.subtract).then_inc(f_lo_ok, 1)
            ffn(0, head=True)
            repeat(dve, 1, KF // 2 - 1, ffn)

            for m in range(KD):
                for j in range(3):
                    u = U_DOWN + 3 * m + j + 1
                    if u < U_END - 1:
                        split_lo(u, u % 2, P * DOWN_K[(j + 1) % 3])
                    elif u == U_END - 1:
                        c = slice(0, P * DOWN_K[2])
                        dve.wait_ge(hi_done, U_END)
                        dve.tensor_tensor(end_lo[:, c], raw[1][:, c], fl(end_hi[:, c]), ALU.subtract).then_inc(lo_done, 1)
                if m + 1 < KD:
                    dve.wait_ge(unit_done, U_DOWN + 3 * m + 3)
                    residual(m, m % 2)
            for half in range(2):
                c, tiles = slice(half * MEM, (half + 1) * MEM), (2 * half, 2 * half + 1)
                dve.wait_ge(end_mm, half + 1)
                dve.tensor_tensor(xT[:, KD - 1, c], ps[END_BANKS[half]][:, 0:MEM], xT[:, KD - 1, c], ALU.add).then_inc(end_ok, 1)
                dve.wait_ge(end_ok, half + 1)
                dve.tensor_scalar(yT[:, 3, c], xT[:, KD - 1, c], gains[:, R_FINAL + KD - 1:R_FINAL + KD], None, ALU.mult).then_inc(y_ok, 1)
                dve.wait_ge(rs_ok, N_X4 + half + 1)
                dve.reciprocal(stat[:, 4 + 2 * half:6 + 2 * half], stat[:, 2 * half:2 * half + 2]).then_inc(y_rs, 1)
                dve.wait_ge(y_rs, half + 1)
                for t in tiles:
                    dve.tensor_scalar(y_nat[:, t, 0:S], y_nat[:, t, 0:S], stat[:, 4 + t:5 + t], None, ALU.mult).then_inc(y_left, 1)


_INS = ["x", "mem", "positions", "g_mix", "w_in", "b_gate", "g_q_lat", "w_uq", "g_kv_lat", "w_ukv", "w_a_proj",
        "w_b_proj", "w_o", "g_x", "g_mem", "w_xq", "w_xkv", "w_xo", "g_ffn", "w_gate", "w_up", "w_down", "g_final"]


def kernel(**inputs):
    import numpy as _np
    import concourse.bacc as _bacc
    from concourse import mybir as _mybir
    from concourse.bass_utils import run_bass_kernel_spmd as _run

    nc = _bacc.Bacc("TRN2", target_bir_lowering=False, num_devices=1)
    freq = (10000.0 ** (-_np.arange(0, ROPE, 2) / ROPE)).astype(_np.float32)
    arrays = {name: _np.ascontiguousarray(inputs[name]) for name in _INS}
    arrays["signed_freq"] = _np.concatenate([-freq, freq]).reshape(ROPE, 1)
    args = [nc.dram_tensor(f"in_{n}", a.shape, _mybir.dt.from_np(a.dtype), kind="ExternalInput").ap() for n, a in arrays.items()]
    args.append(nc.dram_tensor("out_y", (1, S, D), _mybir.dt.float32, kind="ExternalOutput").ap())
    build(nc, *args)
    r = _run(nc, [{f"in_{n}": a for n, a in arrays.items()}], core_ids=[0])
    return r.results[0]["out_y"]
```
